# Optimizing a Trainium2 kernel written in Bass

```python
import math
import jax, jax.numpy as jnp
from jax import lax
import numpy as np

D_MODEL = 2048
BATCH = 1
SEQ = 256
DEPTH = 1

SB_HEADS = 8
SB_HEAD_DIM = 128
SB_WIDTH = SB_HEADS * SB_HEAD_DIM
HG_HEADS = 8
HG_HEAD_DIM = 128
HG_WIDTH = HG_HEADS * HG_HEAD_DIM
D_FF = 4 * D_MODEL
PLE_DIM = 256
Q_BLOCK = 128
HG_CHUNK = 64
EPS = 1e-6

IN_WIDTH = 3 * SB_WIDTH + 4 * HG_WIDTH + 2 * D_MODEL
SPLIT_POINTS = (SB_WIDTH, 2 * SB_WIDTH, 3 * SB_WIDTH, 3 * SB_WIDTH + HG_WIDTH, 3 * SB_WIDTH + 2 * HG_WIDTH, 3 * SB_WIDTH + 3 * HG_WIDTH, 3 * SB_WIDTH + 4 * HG_WIDTH, 3 * SB_WIDTH + 4 * HG_WIDTH + D_MODEL)

kernel_name = 'hybrid_stickbreaking_hgrn2_gated_block'

def rmsnorm(x, g):
    xf = x.astype(jnp.float32)
    var = jnp.mean(xf * xf, axis=-1, keepdims=True)
    return (xf * lax.rsqrt(var + EPS) * g.astype(jnp.float32)).astype(x.dtype)

def split_heads(t, n_heads):
    b, s, w = t.shape
    return t.reshape(b, s, n_heads, w // n_heads).transpose(0, 2, 1, 3)

def merge_heads(t):
    b, h, s, d = t.shape
    return t.transpose(0, 2, 1, 3).reshape(b, s, h * d)

def stick_breaking_attention(q, k, v):
    b, h, s, dh = q.shape
    n_blk = s // Q_BLOCK
    scale = dh ** -0.5
    kf = k.astype(jnp.float32)
    vf = v.astype(jnp.float32)
    key_pos = jnp.arange(s)

    def block(i):
        start = i * Q_BLOCK
        qb = lax.dynamic_slice_in_dim(q, start, Q_BLOCK, axis=2).astype(jnp.float32)
        z = jnp.einsum('bhtd,bhsd->bhts', qb, kf) * scale
        qpos = start + jnp.arange(Q_BLOCK)
        mask = key_pos[None, :] < qpos[:, None]
        log_keep = jnp.where(mask, jax.nn.log_sigmoid(-z), 0.0)
        later = lax.cumsum(log_keep, axis=3, reverse=True) - log_keep
        w = jnp.where(mask, jnp.exp(jax.nn.log_sigmoid(z) + later), 0.0)
        return jnp.einsum('bhts,bhsd->bhtd', w, vf)

    out = lax.map(block, jnp.arange(n_blk))
    out = jnp.transpose(out, (1, 2, 0, 3, 4)).reshape(b, h, s, dh)
    return out.astype(q.dtype)

def hgrn2_chunkwise(q, log_f, k, v):
    b, h, s, dk = q.shape
    dv = v.shape[-1]
    n = s // HG_CHUNK

    def to_chunks(t):
        return jnp.moveaxis(t.reshape(b, h, n, HG_CHUNK, t.shape[-1]), 2, 0)

    qc, gc, kc, vc = to_chunks(q), to_chunks(log_f), to_chunks(k), to_chunks(v)
    causal = jnp.tril(jnp.ones((HG_CHUNK, HG_CHUNK), dtype=bool))

    def step(state, inp):
        qi, gi, ki, vi = inp
        bcum = jnp.cumsum(gi, axis=2)
        diff = bcum[:, :, :, None, :] - bcum[:, :, None, :, :]
        decay = jnp.exp(jnp.where(causal[:, :, None], diff, -jnp.inf))
        scores = jnp.einsum('bhtk,bhtsk,bhsk->bhts', qi, decay, ki)
        o = jnp.einsum('bhts,bhsv->bhtv', scores, vi)
        o = o + jnp.einsum('bhtk,bhkv->bhtv', qi * jnp.exp(bcum), state)
        b_last = bcum[:, :, -1:, :]
        k_dec = ki * jnp.exp(b_last - bcum)
        state = jnp.exp(b_last[:, :, 0, :])[..., None] * state + jnp.einsum('bhsk,bhsv->bhkv', k_dec, vi)
        return state, o

    s0 = jnp.zeros((b, h, dk, dv), jnp.float32)
    _, oc = lax.scan(step, s0, (qc, gc, kc, vc))
    return jnp.moveaxis(oc, 0, 2).reshape(b, h, s, dv)

def hgrn_lower_bounds(lb_logits):
    pr = jax.nn.softmax(lb_logits.astype(jnp.float32), axis=0)
    return jnp.cumsum(pr, axis=0)[:DEPTH]

def headwise_rmsnorm(o, g, n_heads):
    b, s, w = o.shape
    of = o.reshape(b, s, n_heads, w // n_heads).astype(jnp.float32)
    var = jnp.mean(of * of, axis=-1, keepdims=True)
    of = of * lax.rsqrt(var + EPS)
    return of.reshape(b, s, w) * g.astype(jnp.float32)

def setup_inputs(seed: int = 0) -> dict:
    key = jax.random.key(seed)
    ks = jax.random.split(key, 16)
    f32 = jnp.float32

    def nrm(k, shape, scale):
        return jax.random.normal(k, shape, f32) * scale

    return {
        'x': nrm(ks[0], (BATCH, SEQ, D_MODEL), 1.0),
        'p': nrm(ks[1], (DEPTH, BATCH, SEQ, PLE_DIM), 1.0),
        'mix_norm_g': 1.0 + nrm(ks[2], (DEPTH, D_MODEL), 0.1),
        'w_in': nrm(ks[3], (DEPTH, D_MODEL, IN_WIDTH), D_MODEL ** -0.5),
        'hgrn_lb_logits': nrm(ks[4], (DEPTH + 1, HG_WIDTH), 0.5),
        'hgrn_out_norm_g': 1.0 + nrm(ks[5], (DEPTH, HG_WIDTH), 0.1),
        'w_o_sb': nrm(ks[6], (DEPTH, SB_WIDTH, D_MODEL), SB_WIDTH ** -0.5),
        'w_o_hg': nrm(ks[7], (DEPTH, HG_WIDTH, D_MODEL), HG_WIDTH ** -0.5),
        'w_out': nrm(ks[8], (DEPTH, D_MODEL, D_MODEL), D_MODEL ** -0.5),
        'mlp_norm_g': 1.0 + nrm(ks[9], (DEPTH, D_MODEL), 0.1),
        'w_up': nrm(ks[10], (DEPTH, D_MODEL, D_FF), D_MODEL ** -0.5),
        'w_down': nrm(ks[11], (DEPTH, D_FF, D_MODEL), D_FF ** -0.5),
        'w_ple_proj': nrm(ks[12], (DEPTH, PLE_DIM, D_MODEL), PLE_DIM ** -0.5),
        'w_ple_gate': nrm(ks[13], (DEPTH, D_MODEL, D_MODEL), D_MODEL ** -0.5),
        'final_norm_g': 1.0 + nrm(ks[14], (D_MODEL,), 0.1),
    }

def reference(x, p, mix_norm_g, w_in, hgrn_lb_logits, hgrn_out_norm_g, w_o_sb, w_o_hg, w_out, mlp_norm_g, w_up, w_down, w_ple_proj, w_ple_gate, final_norm_g):
    f32 = jnp.float32
    lower_bounds = hgrn_lower_bounds(hgrn_lb_logits)
    for i in range(DEPTH):
        h = rmsnorm(x, mix_norm_g[i])
        proj = h @ w_in[i]
        q_sb, k_sb, v_sb, f_raw, i_hg, q_hg, g_hg, gate_sb, gate_hg = jnp.split(proj, SPLIT_POINTS, axis=-1)

        y_sb = merge_heads(stick_breaking_attention(split_heads(q_sb, SB_HEADS), split_heads(k_sb, SB_HEADS), split_heads(v_sb, SB_HEADS)))

        lb = lower_bounds[i]
        f = lb + (1.0 - lb) * jax.nn.sigmoid(f_raw.astype(f32))
        log_f = jnp.log(f)
        k_hg = 1.0 - f
        q_act = jax.nn.silu(q_hg.astype(f32))
        o_hg = hgrn2_chunkwise(split_heads(q_act, HG_HEADS), split_heads(log_f, HG_HEADS), split_heads(k_hg, HG_HEADS), split_heads(i_hg.astype(f32), HG_HEADS))
        o_hg = merge_heads(o_hg)
        y_hg = (headwise_rmsnorm(o_hg, hgrn_out_norm_g[i], HG_HEADS) * jax.nn.silu(g_hg.astype(f32))).astype(x.dtype)

        y = jax.nn.sigmoid(gate_sb) * (y_sb @ w_o_sb[i]) + jax.nn.sigmoid(gate_hg) * (y_hg @ w_o_hg[i])
        x = x + y @ w_out[i]

        h = rmsnorm(x, mlp_norm_g[i])
        x = x + jnp.square(jax.nn.relu(h @ w_up[i])) @ w_down[i]

        x = x + jax.nn.sigmoid(x @ w_ple_gate[i]) * (p[i] @ w_ple_proj[i])
    return rmsnorm(x, final_norm_g)


_drawn_inputs = setup_inputs


def setup_inputs(seed=0):
    import zlib

    import numpy as np

    out = dict(_drawn_inputs(seed))
    spreads = {}
    factors = {'hgrn_lb_logits': 3.253}
    for name, (base, spread) in spreads.items():
        noise = np.random.default_rng([zlib.crc32(name.encode()), seed]).standard_normal(out[name].shape)
        drawn = base * np.exp(spread * noise) if base else spread * noise
        out[name] = __import__('jax').numpy.asarray(drawn.astype(out[name].dtype))
    for name, factor in factors.items():
        out[name] = (out[name] * factor).astype(out[name].dtype)
    return out
```

```python
from contextlib import ExitStack

import numpy as np

import concourse.bass as bass
from concourse import mybir

F32 = mybir.dt.float32
F32R = mybir.dt.float32r
U8 = mybir.dt.uint8
ACT = mybir.ActivationFunctionType
ALU = mybir.AluOpType
AXX = mybir.AxisListType.X
ds = bass.ds

P = 128
D = 2048
T = 256
TT = T // P
HEADS = 8
HW = HEADS * P
FF = 4 * D
PLE = 256
EPS = 1e-6
SW = 512
KT = D // P
UK = 2
UPS = KT // UK
PAIR = 2 * UPS
RAW = 8
SPL = 4
LEAD = 3
DS = D // SW
QUARTERS = 4
LEVELS = 8

U_QKV, G_QKV = 0, 0
U_HGP, G_HGP = U_QKV + 3 * PAIR, G_QKV + 6
U_GAT, G_GAT = U_HGP + 4 * PAIR, G_HGP + 8
U_WSB, G_WSB = U_GAT + 4 * PAIR, G_GAT + 8
U_WHG, G_WHG = U_WSB + PAIR, G_WSB + DS
U_OUT, G_OUT = U_WHG + PAIR, G_WHG + DS
U_PLE, G_PLE = U_OUT + DS * UPS, G_OUT + DS
U_MLP, G_MLP = U_PLE + DS, G_PLE + DS
QU = 2 * DS * UPS
U_GLU, G_GLU = U_MLP + QUARTERS * QU, G_MLP + QUARTERS * 2 * DS
U_END = U_GLU + DS * UPS

R_X = 0
R_HG = R_X + 8
R_Y = R_HG + 4
R_X1 = R_Y + 8
R_P = R_X1 + 6
R_X1B = R_P + 1
R_U = R_X1B + 2
R_X2 = R_U + QUARTERS * 8

V_F, V_K0, V_Q0 = 1, 2, 3
V_STEPS = 31


def v_t(j):
    return V_F if j == 0 else 3 * j + 1


def v_q(j):
    return V_Q0 if j == 0 else (3 * j + 3 if j < 7 else 23)


def v_s(n):
    return 23 + n


G_STEPS = 14


def build(nc, x, p, g_mix, w_in, lb_logits, g_hg, w_o_sb, w_o_hg, w_out, g_mlp, w_up, w_down,
          w_ple, w_glu, g_fin, c_ident, c_ntri, c_masks, out):
    ctx = ExitStack()
    with ctx:
        def sem(name):
            return ctx.enter_context(nc.semaphore(name))

        at = [(nc.sbuf_base + 63) // 64 * 64]

        def take(n):
            at[0] += n
            return at[0] - n

        def tile(name, shape, dt, offset):
            return nc.alloc_sbuf_tensor_at(name, shape, dt, offset=offset)

        KB = 1024
        raw = tile("raw", [P, RAW, UK, SW], F32, take(32 * KB))
        w_hi = tile("w_hi", [P, SPL, UK, SW], F32R, take(16 * KB))
        w_lo = tile("w_lo", [P, SPL, UK, SW], F32R, take(16 * KB))
        a_hi = tile("a_hi", [P, KT * T], F32R, take(16 * KB))
        a_lo = tile("a_lo", [P, KT * T], F32R, take(16 * KB))
        at_b = take(32 * KB)
        b_hi = tile("b_hi", [P, KT * T], F32R, at_b)
        b_lo = tile("b_lo", [P, KT * T], F32R, at_b + 16 * KB)
        q_lev = tile("q_lev", [P, 8, T], F32, at_b + 8 * KB)
        k_lev = tile("k_lev", [P, 8, T], F32, at_b + 24 * KB)
        masks_in = tile("masks_in", [P, LEVELS * T], F32, at_b + 24 * KB)
        at_1 = take(32 * KB)
        qkv = tile("qkv", [P, TT * 3 * HW], F32, at_1)
        stage = [tile(f"stage{j}", [P, TT, 3, P], F32, at_1 + (24 + 3 * j) * KB) for j in range(2)]
        sb_qT = tile("sb_qT", [P, T], F32, at_1 + 30 * KB)
        sb_kT = tile("sb_kT", [P, T], F32, at_1 + 31 * KB)
        square = tile("square", [P, D], F32, at_1)
        gates = tile("gates", [P, 4 * TT * HW], F32, at_1)
        u_hi = tile("u_hi", [P, KT * T], F32R, at_1)
        u_lo = tile("u_lo", [P, KT * T], F32R, at_1 + 16 * KB)
        square1 = tile("square1", [P, D], F32, at_1 + 8 * KB)
        g_fin_b = tile("g_fin_b", [P, D], F32, at_1)
        square2 = tile("square2", [P, SW], F32, at_1 + 8 * KB)
        at_2 = take(32 * KB)
        x_in = tile("x_in", [P, TT, D], F32, at_2)
        hgp = tile("hgp", [P, 4 * TT * HW], F32, at_2)
        x_res = tile("x_res", [P, TT, D], F32, at_2)
        ple = tile("ple", [P, TT, D], F32, at_2 + 16 * KB)
        ident = tile("ident", [P, P], F32, take(512))
        ntri = tile("ntri", [P, P], F32, take(512))
        nones = tile("nones", [P, P], F32, take(512))
        masks = tile("masks", [P, LEVELS * T], U8, take(LEVELS * T))
        at_g = take(512)
        g_rows = tile("g_rows", [P, P], F32, at_g)
        gT = tile("gT", [P, 64], F32, take(256))
        lb2 = tile("lb2", [P, 2, HEADS], F32, take(64))
        lb_s = tile("lb_s", [P, 4, HEADS], F32, take(128))
        lbT = tile("lbT", [P, 2, HEADS], F32, take(64))
        lb_h = tile("lb_h", [P, 2, 1], F32, take(32))
        stat = tile("stat", [P, 4, 8], F32, take(128))
        stat_h = tile("stat_h", [P, 3, 16], F32, take(192))
        at_s = take(0)
        sp = tile("sp", [P, 3 * P], F32, at_s)
        wt = tile("wt", [P, 3 * P], F32, at_s + 1536)
        s_f = tile("s_f", [P, TT, P], F32, at_s)
        s_qg = tile("s_qg", [P, 2, TT, P], F32, at_s + 1 * KB)
        st_q = tile("st_q", [P, TT, P], F32, at_s + 3 * KB)
        q_dia = tile("q_dia", [P, T], F32, at_s + 4 * KB)
        t_lev = [tile(f"t_lev{j}", [P, T >> j], F32, at_s + 5 * KB + (2 * KB - (2 * KB >> j))) for j in range(7)]
        score = tile("score", [P, T], F32, at_s + 7 * KB)
        cross = tile("cross", [P, P], F32, at_s + 8 * KB)
        un = tile("un", [P, TT, SW], F32, at_s)
        usq = tile("usq", [P, TT, SW], F32, at_s + 4 * KB)
        p_in = tile("p_in", [P, TT, PLE], F32, at_s)
        assert at_s + 8 * KB + 512 <= nc.sbuf_usable_end

        acc = ctx.enter_context(nc.psum_tensor("acc", [P, 4, SW], F32))
        side = ctx.enter_context(nc.psum_tensor("side", [P, 4, SW], F32))

        raw_full = [sem(f"raw_full{s}") for s in range(RAW)]
        hi_done = sem("hi_done")
        lo_done = sem("lo_done")
        units_used = sem("units_used")
        free0 = sem("free0")
        free1 = sem("free1")
        tr_full = sem("tr_full")
        tr_hi = sem("tr_hi")
        tr_lo = sem("tr_lo")
        ident_in, x_half, tables_in = sem("ident_in"), [sem("x_half0"), sem("x_half1")], sem("tables_in")
        g_zero, g_in, g_turned, g_ready = sem("g_zero"), sem("g_in"), sem("g_turned"), sem("g_ready")
        xres_in, p_in_s, gfin_in, stored = sem("xres_in"), sem("p_in_s"), sem("gfin_in"), sem("stored")
        preset = sem("preset")
        rms_sum, rms_inv, rms_ready = sem("rms_sum"), sem("rms_inv"), sem("rms_ready")
        rms_mean = sem("rms_mean")
        lb_vec, lb_exp = sem("lb_vec"), sem("lb_exp")
        sb_staged, sb_turned, sb_q, sb_k = sem("sb_staged"), sem("sb_turned"), sem("sb_q"), sem("sb_k")
        sb_z, sb_soft, sb_keep, sb_masked = sem("sb_z"), sem("sb_soft"), sem("sb_keep"), sem("sb_masked")
        sb_later, sb_w, sb_wm = sem("sb_later"), sem("sb_w"), sem("sb_wm")
        sb_o, sb_hi, sb_lo = sem("sb_o"), sem("sb_hi"), sem("sb_lo")
        hg_sig, hg_prep, hg_turned, hg_q = sem("hg_sig"), sem("hg_prep"), sem("hg_turned"), sem("hg_q")
        hg_vec, hg_key, hg_s1, hg_s2 = sem("hg_vec"), sem("hg_key"), sem("hg_s1"), sem("hg_s2")
        hg_cross, hg_o, hg_out = sem("hg_cross"), sem("hg_o"), sem("hg_out")
        hn_sq, hn_mean, hn_inv, hn_rstd, hn_mul, hn_y = (sem("hn_sq"), sem("hn_mean"), sem("hn_inv"),
                                                         sem("hn_rstd"), sem("hn_mul"), sem("hn_y"))
        y_ready, usq_done = sem("y_ready"), sem("usq_done")
        glu_sig, glu_mul, glu_sum = sem("glu_sig"), sem("glu_mul"), sem("glu_sum")
        fin_scaled, fin_ready = sem("fin_scaled"), [sem("fin_ready0"), sem("fin_ready1"), sem("fin_ready2")]

        qkv_v = qkv[:, :].rearrange("p (t k c) -> p t k c", t=TT, k=3)
        hgp_v = hgp[:, :].rearrange("p (k t c) -> p k t c", k=4, t=TT)
        hgf = hgp[:, 0:TT * HW]
        hgo = hgp[:, TT * HW:2 * TT * HW]
        hgy = hgp[:, 2 * TT * HW:3 * TT * HW]
        hgg = hgp[:, 3 * TT * HW:4 * TT * HW]

        def gate(kind, k):
            return gates[:, :].rearrange("p (i t c) -> p i t c", i=4, t=TT)[:, 2 * kind + k // 2, :,
                                                                           k % 2 * SW:k % 2 * SW + SW]

        def even_odd(row, m):
            v = row.rearrange("p (b two m) -> p b two m", two=2, m=m)
            return v[:, :, 0, :], v[:, :, 1, :]

        def totals(j):
            n = T >> (j + 1)
            v = t_lev[j][:, :].rearrange("p (b two) -> p b two", two=2)
            return (v[:, :, 0:1].to_broadcast([P, n, 1 << j]), v[:, :, 1:2].to_broadcast([P, n, 1 << j]))

        def upper(t):
            return t[:, :].rearrange("p (b c) -> p b c", b=3)[:, 0:3:2, :]

        block = ctx.enter_context(nc.Block())

        @block.sync
        def _(spe):
            def load(n, us, src):
                if us >= RAW:
                    spe.wait_ge(lo_done, n - (RAW - 1))
                spe.dma_start(raw[:, us % RAW, :, :], src).then_inc(raw_full[us % RAW], 16)

            def part(w, row, col):
                return w[ds(row, UK * P), ds(col, SW)].rearrange("(k q) n -> q k n", q=P)

            def in_pair(i, first):
                for u in range(PAIR):
                    load(i * PAIR + u, u + (0 if first else RAW), part(w_in, u % UPS * UK * P, i * 2 * SW + u // UPS * SW))

            spe.dma_start(ident[:, :], c_ident).then_inc(ident_in, 16)
            xv = x.rearrange("(t p) n -> p t n", p=P)
            for c in range(2):
                spe.dma_start(x_in[:, :, c * HW:(c + 1) * HW], xv[:, :, c * HW:(c + 1) * HW]).then_inc(x_half[c], 16)
            in_pair(0, True)
            with spe.Fori(1, 11) as i:
                in_pair(i, False)
            for w, base in ((w_o_sb, U_WSB), (w_o_hg, U_WHG)):
                for u in range(PAIR):
                    load(base + u, base + u, part(w, u % 4 * UK * P, u // 4 * SW))
            spe.wait_ge(hn_y, 1)
            spe.wait_ge(tr_lo, R_Y)
            spe.dma_start(x_res[:, :, :], xv).then_inc(xres_in, 16)
            spe.dma_start(p_in[:, :, :], p.rearrange("(t p) n -> p t n", p=P)).then_inc(p_in_s, 16)
            for u in range(DS * UPS):
                load(U_OUT + u, U_OUT + u, part(w_out, u % UPS * UK * P, u // UPS * SW))
            for u in range(DS):
                load(U_PLE + u, U_PLE + u, part(w_ple, 0, u * SW))
            with spe.Fori(0, QUARTERS) as q:
                for u in range(DS * UPS):
                    load(q * QU + (U_MLP + u), U_MLP + u, part(w_up, u % UPS * UK * P, q * D + u // UPS * SW))
                for u in range(DS * UPS):
                    v = DS * UPS + u
                    load(q * QU + (U_MLP + v), U_MLP + v, part(w_down, q * D + u % UPS * UK * P, u // UPS * SW))
            for u in range(DS * UPS):
                load(U_GLU + u, U_GLU + u, part(w_glu, u % UPS * UK * P, u // UPS * SW))
            spe.wait_ge(units_used, U_GLU)
            spe.dma_start(g_fin_b[:, :], g_fin.partition_broadcast(P)).then_inc(gfin_in, 16)
            ov = out.rearrange("(t p) n -> p t n", p=P)
            for s, (t, c) in enumerate(((1, 0), (0, 0), (0, 1), (1, 1))):
                spe.wait_ge(fin_ready[0 if s == 0 else 1], max(s, 1))
                spe.dma_start(ov[:, t, c * HW:(c + 1) * HW], x_res[:, t, c * HW:(c + 1) * HW]).then_inc(stored, 16)
            spe.wait_ge(stored, 64)

        @block.gpsimd
        def _(pool):
            nc.gpsimd.memset(g_rows[:, :], 0.0).then_inc(g_zero, 1)
            nc.gpsimd.memset(nones[:, :], -1.0).then_inc(preset, 1)

            pool.wait_ge(tables_in, 32)
            nc.gpsimd.tensor_copy(masks[:, :], masks_in[:, :]).then_inc(preset, 1)

            def staged(h, i, j):
                pool.wait_ge(free0, i + 5)
                pool.wait_ge(free1, i + 5)
                pool.wait_ge(units_used, (h + 5) * UPS)
                nc.gpsimd.tensor_copy(stage[j][:, :, :, :], qkv_v[:, :, :, ds(h * P, P)]).then_inc(sb_staged, 1)

            def keep_earlier(tl):
                pool.nop(nofuse=True)
                return nc.gpsimd.affine_select(out=upper(tl), in_=upper(tl), compare_op=ALU.is_gt, fill=0.0,
                                               base=0, pattern=[[0, 2], [1, P]], channel_multiplier=-1)

            with pool.Fori(0, 4) as i:
                for j in range(2):
                    h = i * 2 + j
                    staged(h, i, j)
                    pool.wait_ge(sb_keep, h + 1)
                    keep_earlier(sp).then_inc(sb_masked, 1)
                    pool.wait_ge(sb_w, h + 1)
                    keep_earlier(wt).then_inc(sb_wm, 1)

            pool.wait_ge(sb_o, HEADS)
            pool.wait_ge(lb_vec, 6)
            nc.gpsimd.memset(score[:, :], 0.0).then_inc(preset, 1)
            with pool.Fori(0, 4) as i:
                for j in range(2):
                    h = i * 2 + j
                    pool.wait_ge(hg_sig, h + 1)
                    nc.gpsimd.tensor_copy(lb_h[:, :, :], lbT[:, :, ds(h, 1)])
                    nc.gpsimd.tensor_tensor(st_q[:, :, :], s_qg[:, 0, :, :], hgp_v[:, 2, :, ds(h * P, P)],
                                            ALU.mult).then_inc(hg_prep, 1)
                    nc.gpsimd.tensor_tensor(hgp_v[:, 3, :, ds(h * P, P)], s_qg[:, 1, :, :],
                                            hgp_v[:, 3, :, ds(h * P, P)], ALU.mult).then_inc(hg_prep, 1)
                    for lev in range(7):
                        pool.wait_ge(hg_vec, h * V_STEPS + max(v_t(lev), V_K0 if lev == 0 else 0))
                        if lev:
                            pool.wait_ge(hg_key, h * G_STEPS + 2 * lev)
                        src, dst = (even_odd(k_lev[:, lv, :], 1 << lev) for lv in (lev, lev + 1))
                        nc.gpsimd.tensor_tensor(dst[0], src[0], totals(lev)[1], ALU.mult).then_inc(hg_key, 1)
                        nc.gpsimd.tensor_copy(dst[1], src[1]).then_inc(hg_key, 1)

            pool.wait_ge(hn_mul, 1)
            nc.gpsimd.tensor_tensor(hgy, hgy, hgg, ALU.mult).then_inc(hn_y, 1)
            for k in range(DS):
                pool.wait_ge(free1, G_WHG + k + 1)
                nc.gpsimd.tensor_tensor(gate(0, k), gate(0, k), gate(1, k), ALU.add).then_inc(y_ready, 1)
            with pool.Fori(0, QUARTERS) as q:
                for k in range(DS):
                    pool.wait_ge(free1, q * 2 * DS + (G_MLP + k + 1))
                    pool.wait_ge(tr_full, q * 8 + (R_U + 2 * k))
                    nc.gpsimd.tensor_tensor(usq[:, :, :], un[:, :, :], un[:, :, :], ALU.mult).then_inc(usq_done, 1)
            pool.wait_ge(gfin_in, 16)
            pool.wait_ge(fin_scaled, 1)
            nc.gpsimd.tensor_tensor(x_res[:, 1, 0:HW], x_res[:, 1, 0:HW], g_fin_b[:, 0:HW],
                                    ALU.mult).then_inc(fin_ready[0], 1)

        @block.scalar
        def _(act):
            def split(us, i=0, step=0):
                act.wait_ge(raw_full[us % RAW], i * (16 * step // RAW) + 16 * (us // RAW + 1))
                if us >= SPL or step:
                    act.wait_ge(units_used, i * step + (us - SPL + 1))
                nc.scalar.activation(w_hi[:, us % SPL, :, :], raw[:, us % RAW, :, :], ACT.Copy).then_inc(hi_done, 1)

            def evac(dst, used, par, t, func, **kw):
                act.wait_ge(units_used, used)
                nc.scalar.activation(dst, acc[:, 2 * par + t, :], func, **kw).then_inc((free0, free1)[t], 1)

            def turned(r, dst, col=None, kt=0):
                act.wait_ge(tr_full, r + 1)
                b = r % 4
                if col is None:
                    nc.scalar.activation(dst[:, kt * T:(kt + 2) * T], side[:, b, :], ACT.Copy).then_inc(tr_hi, 1)
                    return
                for kk in range(2):
                    ins = nc.scalar.activation(dst[:, (kt + kk) * T:(kt + kk + 1) * T], side[:, b, kk * T:(kk + 1) * T],
                                               ACT.Copy, scale=gT[:, col + kt + kk:col + kt + kk + 1])
                ins.then_inc(tr_hi, 1)

            act.wait_ge(g_zero, 1)
            for s, (g, k) in enumerate(((g_mix, KT), (g_mlp, KT), (g_hg, HEADS), (lb_logits, 2 * HEADS))):
                row = (0, KT, 2 * KT, 2 * KT + HEADS)[s]
                act.dma_start(g_rows[row:row + k, :], g.rearrange("a (k p) -> (a k) p", p=P)).then_inc(g_in, 16)
            act.dma_start(ntri[:, :], c_ntri).then_inc(tables_in, 16)
            act.dma_start(masks_in[:, :], c_masks).then_inc(tables_in, 16)
            act.wait_ge(g_ready, 1)
            turned(0, a_hi, 0, 0)
            turned(1, a_hi, 0, 2)
            split(0)
            turned(2, a_hi, 0, 4)
            split(1)
            turned(3, a_hi, 0, 6)
            split(2)

            def qkv_evac(i, j):
                evac(qkv[:, ds(i * HW + j * SW, SW)], i * PAIR + (j + 1) * UPS, j, 0,
                     ACT.Copy, scale=stat[:, 0, 6:7])

            for u in range(PAIR):
                split(u + LEAD)
                if u < 4:
                    turned(4 + u, a_hi, 0, 8 + 2 * u)
                if u == 3:
                    for t in range(TT):
                        ins = nc.scalar.activation(square[:, :], x_in[:, t, :], ACT.Square, accum_out=stat[:, 0, t:t + 1])
                        ins.then_inc(rms_sum, 1)
                        act.wait_ge(rms_sum, t + 1)
                if u == 4:
                    act.wait_ge(rms_inv, 1)
                    nc.scalar.activation(stat[:, 0, 6:8], stat[:, 0, 4:6], ACT.Sqrt).then_inc(rms_ready, 1)
                    act.wait_ge(rms_ready, 1)
                if u == 5:
                    act.wait_ge(lb_vec, 2)
                    nc.scalar.activation(lb_s[:, 0:2, :], lb2[:, :, :], ACT.Exp).then_inc(lb_exp, 1)
                if u % UPS == UPS - 1:
                    qkv_evac(0, u // UPS)
            with act.Fori(1, 3) as i:
                for u in range(PAIR):
                    split(u + LEAD, i, PAIR)
                    if u % UPS == UPS - 1:
                        qkv_evac(i, u // UPS)

            with act.Fori(0, 4) as i:
                for j in range(2):
                    h = i * 2 + j
                    act.wait_ge(sb_turned, h + 1)
                    nc.scalar.activation(sb_qT[:, :], side[:, 0, 0:T], ACT.Copy, scale=float(P) ** -0.5).then_inc(sb_q, 1)
                    for u in range(UPS):
                        v = U_HGP + j * UPS + u
                        split(v + LEAD, i, PAIR)
                        if u == 0:
                            act.wait_ge(sb_z, h + 1)
                            nc.scalar.activation(sp[:, :], side[:, 1, 0:3 * P], ACT.Abs).then_inc(sb_soft, 1)
                            act.wait_ge(sb_soft, h * 3 + 1)
                            nc.scalar.activation(sp[:, :], sp[:, :], ACT.Exp, scale=-1.0).then_inc(sb_soft, 1)
                            act.wait_ge(sb_soft, h * 3 + 2)
                            nc.scalar.activation(sp[:, :], sp[:, :], ACT.Ln, bias=1.0).then_inc(sb_soft, 1)
                        if u == 2:
                            act.wait_ge(sb_later, h + 1)
                            nc.scalar.activation(wt[:, :], side[:, 1, 0:3 * P], ACT.Exp).then_inc(sb_w, 1)
                        if u == 4:
                            act.wait_ge(sb_o, h + 1)
                            nc.scalar.activation(b_hi[:, ds(h * T, T)], side[:, 3, 0:T], ACT.Copy).then_inc(sb_hi, 1)
                    evac(hgp[:, ds(i * TT * HW + j * SW, SW)], i * PAIR + (U_HGP + (j + 1) * UPS), j, 0,
                         ACT.Copy, scale=stat[:, 0, 6:7])

            with act.Fori(0, 4) as i:
                for j in range(2):
                    h = i * 2 + j
                    if j == 0:
                        act.wait_ge(free1, i + (G_GAT - 1))
                    nc.scalar.activation(s_f[:, :, :], hgp_v[:, 0, :, ds(h * P, P)], ACT.Sigmoid)
                    nc.scalar.activation(s_qg[:, :, :, :], hgp_v[:, 2:4, :, ds(h * P, P)], ACT.Sigmoid).then_inc(hg_sig, 1)
                    for u in range(UPS):
                        v = U_GAT + j * UPS + u
                        split(v + LEAD, i, PAIR)
                        if u == 0:
                            act.wait_ge(hg_turned, h + 1)
                            nc.scalar.activation(q_dia[:, :], side[:, 0, T:2 * T], ACT.Copy).then_inc(hg_q, 1)
                        if u == 5:
                            act.wait_ge(hg_s2, h + 1)
                            nc.scalar.activation(cross[:, :], side[:, 1, 0:P], ACT.Copy).then_inc(hg_cross, 1)
                        if u == 7:
                            act.wait_ge(hg_o, h + 1)
                            nc.scalar.activation(hgp_v[:, 1, :, ds(h * P, P)],
                                                 side[:, 2, 0:T].rearrange("p (t c) -> p t c", t=TT),
                                                 ACT.Copy).then_inc(hg_out, 1)
                    for t in range(TT):
                        evac(gates[:, ds(i * TT * HW + t * HW + j * SW, SW)], i * PAIR + (U_GAT + (j + 1) * UPS), j, t,
                             ACT.Sigmoid, scale=stat[:, 0, 6 + t:7 + t])

            def splits(base, u):
                if base + u + LEAD < U_END:
                    split(base + u + LEAD)

            for u in range(PAIR):
                splits(U_WSB, u)
                if u == 0:
                    act.wait_ge(hg_out, HEADS)
                    nc.scalar.activation(hgf, hgo, ACT.Square).then_inc(hn_sq, 1)
                if u == 3:
                    act.wait_ge(hn_inv, 1)
                    nc.scalar.activation(stat_h[:, 2, :], stat_h[:, 1, :], ACT.Sqrt).then_inc(hn_rstd, 1)
                if 9 <= u < 13:
                    turned(R_HG + u - 9, b_hi, 2 * KT - HEADS, HEADS + 2 * (u - 9))
            for u in range(PAIR):
                splits(U_WHG, u)
                if u in (6, 10, 14):
                    k = (u - 6) // 4
                    for b in range(2):
                        turned(R_Y + 2 * k + b, a_hi, None, 4 * k + 2 * b)
            for u in range(DS * UPS):
                splits(U_OUT, u)
                if u == 2:
                    for b in range(2):
                        turned(R_Y + 6 + b, a_hi, None, 12 + 2 * b)
                if u in (10, 18, 26):
                    k = (u - 10) // 8
                    for b in range(2):
                        turned(R_X1 + 2 * k + b, b_hi, KT, 4 * k + 2 * b)
                if u == 28:
                    turned(R_P, u_hi)
            for u in range(DS):
                splits(U_PLE, u)
                if u == 1:
                    for b in range(2):
                        turned(R_X1B + b, b_hi, KT, 12 + 2 * b)
                evac(ple[:, 0, u * SW:(u + 1) * SW], U_PLE + u + 1, u % 2, 0, ACT.Copy)
                if u >= 2:
                    act.wait_ge(rms_sum, u)
                    nc.scalar.activation(square1[:, :], x_res[:, u - 2, :], ACT.Square,
                                         accum_out=stat[:, 1, u - 2:u - 1]).then_inc(rms_sum, 1)
            act.wait_ge(rms_inv, 2)
            nc.scalar.activation(stat[:, 1, 6:8], stat[:, 1, 4:6], ACT.Sqrt).then_inc(rms_ready, 1)
            act.wait_ge(rms_ready, 2)
            with act.Fori(0, QUARTERS) as q:
                for u in range(QU):
                    v = U_MLP + u
                    split(v + LEAD, q, QU)
                    if u % UPS == UPS - 1 and u < DS * UPS:
                        k = u // UPS
                        for t in range(TT):
                            evac(un[:, t, :], q * QU + (v + 1), k % 2, t, ACT.Relu, scale=stat[:, 1, 6 + t:7 + t])
                    if u % UPS == 2 and UPS < u < DS * UPS + UPS:
                        k = u // UPS - 1
                        for b in range(2):
                            act.wait_ge(tr_full, q * 8 + (R_U + 2 * k + b + 1))
                            nc.scalar.activation(u_hi[:, (4 * k + 2 * b) * T:(4 * k + 2 * b + 2) * T],
                                                 side[:, (R_U + 2 * k + b) % 4, :], ACT.Copy).then_inc(tr_hi, 1)
            for b in range(4):
                turned(R_X2 + b, a_hi, None, 2 * b)
            for u in range(DS * UPS):
                splits(U_GLU, u)
                if u < 4:
                    turned(R_X2 + 4 + u, a_hi, None, 8 + 2 * u)
                if u % UPS == UPS - 1:
                    k = u // UPS
                    act.wait_ge(units_used, U_GLU + u + 1)
                    if k >= 2:
                        act.wait_ge(glu_sum, k - 1)
                    sg = (un, usq)[k % 2]
                    nc.scalar.activation(sg[:, :, :], acc[:, 2 * (k % 2):2 * (k % 2) + 2, :], ACT.Sigmoid).then_inc(glu_sig, 1)
                if u % UPS == 2 and u > UPS or u == DS * UPS - 1:
                    for k in ([u // UPS - 1] if u < DS * UPS - 1 else [DS - 1]):
                        act.wait_ge(glu_sum, k + 1)
                        for t in range(TT):
                            if k or t:
                                act.wait_ge(rms_sum, 4 + TT * k + t)
                            nc.scalar.activation(square2[:, :], x_res[:, t, k * SW:(k + 1) * SW], ACT.Square,
                                                 accum_out=stat[:, 2 + t, k:k + 1]).then_inc(rms_sum, 1)
            act.wait_ge(rms_inv, 3)
            nc.scalar.activation(stat[:, 2, 6:8], stat[:, 2, 4:6], ACT.Sqrt).then_inc(rms_ready, 1)
            act.wait_ge(rms_ready, 3)
            nc.scalar.activation(x_res[:, 1, 0:HW], x_res[:, 1, 0:HW], ACT.Copy, scale=stat[:, 2, 7:8]).then_inc(fin_scaled, 1)

        @block.vector
        def _(dve):
            def split(us, i=0, step=0):
                dve.wait_ge(hi_done, i * step + (us + 1))
                nc.vector.tensor_tensor(w_lo[:, us % SPL, :, :], raw[:, us % RAW, :, :],
                                        w_hi[:, us % SPL, :, :].bitcast(F32), ALU.subtract).then_inc(lo_done, 1)

            def turned(r, hi, lo, col=None, kt=0):
                dve.wait_ge(tr_hi, r + 1)
                b = r % 4
                for kk in range(2):
                    if col is None and kk:
                        break
                    n = 2 * T if col is None else T
                    a = (kt + kk) * T
                    src = side[:, b, kk * T:kk * T + n]
                    if col is None:
                        ins = nc.vector.tensor_tensor(lo[:, a:a + n], src, hi[:, a:a + n].bitcast(F32), ALU.subtract)
                    else:
                        c = col + kt + kk
                        ins = nc.vector.scalar_tensor_tensor(out=lo[:, a:a + n], in0=src, scalar=gT[:, c:c + 1],
                                                             in1=hi[:, a:a + n].bitcast(F32), op0=ALU.mult, op1=ALU.subtract)
                ins.then_inc(tr_lo, 1)

            def inverse_mean(row, n):
                nc.vector.tensor_scalar(stat[:, row, 2:4], stat[:, row, 0:2], 1.0 / D, EPS,
                                        ALU.mult, ALU.add).then_inc(rms_mean, 1)
                dve.wait_ge(rms_mean, n)
                nc.vector.reciprocal(stat[:, row, 4:6], stat[:, row, 2:4]).then_inc(rms_inv, 1)

            def gated(base, kind, k):
                dve.wait_ge(units_used, base + 4 * (k + 1))
                for t in range(TT):
                    nc.vector.tensor_tensor(gate(kind, k)[:, t, :], acc[:, 2 * (k % 2) + t, :], gate(kind, k)[:, t, :],
                                            ALU.mult).then_inc((free0, free1)[t], 1)

            def added(used, k):
                dve.wait_ge(units_used, used)
                for t in range(TT):
                    xs = x_res[:, t, k * SW:(k + 1) * SW]
                    nc.vector.tensor_tensor(xs, acc[:, 2 * (k % 2) + t, :], xs, ALU.add).then_inc((free0, free1)[t], 1)

            dve.wait_ge(g_turned, 1)
            nc.vector.tensor_copy(gT[:, :], acc[:, 3, 0:64]).then_inc(g_ready, 1)
            dve.wait_ge(g_ready, 1)
            turned(0, a_hi, a_lo, 0, 0)
            turned(1, a_hi, a_lo, 0, 2)
            split(0)
            turned(2, a_hi, a_lo, 0, 4)
            split(1)
            turned(3, a_hi, a_lo, 0, 6)
            split(2)

            def qkv_evac(i, j):
                dve.wait_ge(units_used, i * PAIR + (j + 1) * UPS)
                nc.vector.tensor_scalar(qkv[:, ds(i * HW + (3 * HW + j * SW), SW)], acc[:, 2 * j + 1, :],
                                        stat[:, 0, 7:8], None, ALU.mult).then_inc(free1, 1)

            for u in range(PAIR):
                split(u + LEAD)
                if u < 4:
                    turned(4 + u, a_hi, a_lo, 0, 8 + 2 * u)
                if u == 4:
                    dve.wait_ge(rms_sum, 2)
                    inverse_mean(0, 1)
                    l0, l1 = gT[:, 40:48], gT[:, 48:56]
                    nc.vector.tensor_tensor(lb_s[:, 2, :], l0, l1, ALU.max).then_inc(lb_vec, 1)
                    dve.wait_ge(lb_vec, 1)
                    nc.vector.tensor_tensor(lb2[:, 0, :], l0, lb_s[:, 2, :], ALU.subtract)
                    nc.vector.tensor_tensor(lb2[:, 1, :], l1, lb_s[:, 2, :], ALU.subtract).then_inc(lb_vec, 1)
                if u == 6:
                    dve.wait_ge(lb_exp, 1)
                    nc.vector.tensor_tensor(lb_s[:, 2, :], lb_s[:, 0, :], lb_s[:, 1, :], ALU.add).then_inc(lb_vec, 1)
                    dve.wait_ge(lb_vec, 3)
                    nc.vector.reciprocal(lb_s[:, 3, :], lb_s[:, 2, :]).then_inc(lb_vec, 1)
                    dve.wait_ge(lb_vec, 4)
                    nc.vector.tensor_tensor(lbT[:, 0, :], lb_s[:, 0, :], lb_s[:, 3, :], ALU.mult).then_inc(lb_vec, 1)
                    dve.wait_ge(lb_vec, 5)
                    nc.vector.tensor_scalar(lbT[:, 1, :], lbT[:, 0, :], -1.0, 1.0, ALU.mult, ALU.add).then_inc(lb_vec, 1)
                if u == 7:
                    dve.wait_ge(rms_ready, 1)
                if u % UPS == UPS - 1:
                    qkv_evac(0, u // UPS)
            with dve.Fori(1, 3) as i:
                for u in range(PAIR):
                    split(u + LEAD, i, PAIR)
                    if u % UPS == UPS - 1:
                        qkv_evac(i, u // UPS)

            with dve.Fori(0, 4) as i:
                for j in range(2):
                    h = i * 2 + j
                    dve.wait_ge(sb_q, h + 1)
                    nc.vector.tensor_copy(sb_kT[:, :], side[:, 0, T:2 * T]).then_inc(sb_k, 1)
                    for u in range(UPS):
                        v = U_HGP + j * UPS + u
                        split(v + LEAD, i, PAIR)
                        if u == 0:
                            dve.wait_ge(sb_soft, h * 3 + 3)
                            nc.vector.scalar_tensor_tensor(out=sp[:, :], in0=side[:, 1, 0:3 * P], scalar=0.0, in1=sp[:, :],
                                                           op0=ALU.max, op1=ALU.add).then_inc(sb_keep, 1)
                        if u == 4:
                            dve.wait_ge(sb_hi, h + 1)
                            nc.vector.tensor_tensor(b_lo[:, ds(h * T, T)], side[:, 3, 0:T],
                                                    b_hi[:, ds(h * T, T)].bitcast(F32), ALU.subtract).then_inc(sb_lo, 1)
                    dve.wait_ge(units_used, i * PAIR + (U_HGP + (j + 1) * UPS))
                    nc.vector.tensor_scalar(hgp[:, ds(i * TT * HW + (HW + j * SW), SW)], acc[:, 2 * j + 1, :],
                                            stat[:, 0, 7:8], None, ALU.mult).then_inc(free1, 1)

            dve.wait_ge(preset, 3)
            with dve.Fori(0, 4) as i:
                for j in range(2):
                    h = i * 2 + j
                    v0 = h * V_STEPS

                    def take_scores(bank, pos, level, n):
                        dve.wait_ge(hg_vec, v0 + v_s(n) - 1)
                        dve.nop(nofuse=True)
                        nc.vector.copy_predicated(score[:, :], masks[:, level * T:(level + 1) * T],
                                                  side[:, bank, pos * T:(pos + 1) * T]).then_inc(hg_vec, 1)

                    for u in range(UPS):
                        v = U_GAT + j * UPS + u
                        split(v + LEAD, i, PAIR)
                        if u == 0:
                            dve.wait_ge(hg_q, h + 1)
                            dve.wait_ge(hg_prep, h * 2 + 1)
                            nc.vector.tensor_scalar(t_lev[0][:, :], side[:, 0, 0:T], lb_h[:, 1, :], lb_h[:, 0, :],
                                                    ALU.mult, ALU.add).then_inc(hg_vec, 1)
                            dve.wait_ge(hg_vec, v0 + V_F)
                            nc.vector.tensor_scalar(k_lev[:, 0, :], t_lev[0][:, :], -1.0, 1.0,
                                                    ALU.mult, ALU.add).then_inc(hg_vec, 1)
                            nc.vector.tensor_tensor(q_lev[:, 0, :], side[:, 0, T:2 * T], t_lev[0][:, :],
                                                    ALU.mult).then_inc(hg_vec, 1)
                            for lev in range(7):
                                dve.wait_ge(hg_vec, v0 + v_q(lev))
                                if lev < 6:
                                    tv = t_lev[lev][:, :].rearrange("p (b two) -> p b two", two=2)
                                    nc.vector.tensor_tensor(t_lev[lev + 1][:, :].unsqueeze(2), tv[:, :, 0:1], tv[:, :, 1:2],
                                                            ALU.mult).then_inc(hg_vec, 1)
                                src, dst = (even_odd(q_lev[:, lv, :], 1 << lev) for lv in (lev, lev + 1))
                                nc.vector.tensor_tensor(dst[1], src[1], totals(lev)[0], ALU.mult).then_inc(hg_vec, 1)
                                nc.vector.tensor_copy(dst[0], src[0]).then_inc(hg_vec, 1)
                        if u == 2:
                            dve.wait_ge(hg_s1, h + 1)
                            for n in range(4):
                                take_scores(1 + n // 2, n % 2, n, n + 1)
                        if u == 5:
                            dve.wait_ge(hg_s2, h + 1)
                            for n in range(4, 8):
                                take_scores((3, 0)[(n - 4) // 2], n % 2, n, n + 1)

            def splits(base, u):
                if base + u + LEAD < U_END:
                    split(base + u + LEAD)

            for u in range(PAIR):
                splits(U_WSB, u)
                if u == 1:
                    dve.wait_ge(hn_sq, 1)
                    nc.vector.tensor_reduce(stat_h[:, 0, :], hgf.rearrange("p (g c) -> p g c", c=P), AXX,
                                            ALU.add).then_inc(hn_mean, 1)
                    dve.wait_ge(hn_mean, 1)
                    nc.vector.tensor_scalar(stat_h[:, 0, :], stat_h[:, 0, :], 1.0 / P, EPS, ALU.mult, ALU.add).then_inc(hn_mean, 1)
                    dve.wait_ge(hn_mean, 2)
                    nc.vector.reciprocal(stat_h[:, 1, :], stat_h[:, 0, :]).then_inc(hn_inv, 1)
                if u == 4:
                    dve.wait_ge(hn_rstd, 1)
                    nc.vector.tensor_tensor(hgy.rearrange("p (g c) -> p g c", c=P), hgo.rearrange("p (g c) -> p g c", c=P),
                                            stat_h[:, 2, :].unsqueeze(2).to_broadcast([P, TT * HEADS, P]),
                                            ALU.mult).then_inc(hn_mul, 1)
                if 9 <= u < 13:
                    turned(R_HG + u - 9, b_hi, b_lo, 2 * KT - HEADS, HEADS + 2 * (u - 9))
                if u % 4 == 3:
                    gated(U_WSB, 0, u // 4)
            for u in range(PAIR):
                splits(U_WHG, u)
                if u in (6, 10, 14):
                    k = (u - 6) // 4
                    for b in range(2):
                        turned(R_Y + 2 * k + b, a_hi, a_lo, None, 4 * k + 2 * b)
                if u % 4 == 3:
                    gated(U_WHG, 1, u // 4)
            for u in range(DS * UPS):
                splits(U_OUT, u)
                if u == 2:
                    for b in range(2):
                        turned(R_Y + 6 + b, a_hi, a_lo, None, 12 + 2 * b)
                if u in (10, 18, 26):
                    k = (u - 10) // 8
                    for b in range(2):
                        turned(R_X1 + 2 * k + b, b_hi, b_lo, KT, 4 * k + 2 * b)
                if u == 28:
                    turned(R_P, u_hi, u_lo)
                if u % UPS == UPS - 1:
                    if u < UPS:
                        dve.wait_ge(xres_in, 16)
                    added(U_OUT + u + 1, u // UPS)
            for u in range(DS):
                splits(U_PLE, u)
                if u == 1:
                    for b in range(2):
                        turned(R_X1B + b, b_hi, b_lo, KT, 12 + 2 * b)
                dve.wait_ge(units_used, U_PLE + u + 1)
                nc.vector.tensor_copy(ple[:, 1, u * SW:(u + 1) * SW], acc[:, 2 * (u % 2) + 1, :]).then_inc(free1, 1)
            dve.wait_ge(rms_sum, 4)
            inverse_mean(1, 2)
            with dve.Fori(0, QUARTERS) as q:
                for u in range(QU):
                    v = U_MLP + u
                    split(v + LEAD, q, QU)
                    if u % UPS == 2 and UPS < u < DS * UPS + UPS:
                        k = u // UPS - 1
                        for b in range(2):
                            a, r = (4 * k + 2 * b) * T, R_U + 2 * k + b
                            dve.wait_ge(tr_hi, q * 8 + (r + 1))
                            nc.vector.tensor_tensor(u_lo[:, a:a + 2 * T], side[:, r % 4, :], u_hi[:, a:a + 2 * T].bitcast(F32),
                                                    ALU.subtract).then_inc(tr_lo, 1)
                    if u % UPS == UPS - 1 and u >= DS * UPS:
                        added(q * QU + (v + 1), u // UPS - DS)
            for b in range(4):
                turned(R_X2 + b, a_hi, a_lo, None, 2 * b)
            for u in range(DS * UPS):
                splits(U_GLU, u)
                if u < 4:
                    turned(R_X2 + 4 + u, a_hi, a_lo, None, 8 + 2 * u)
                if u % UPS == UPS - 1:
                    k = u // UPS
                    sg = (un, usq)[k % 2]
                    xs = x_res[:, :, k * SW:(k + 1) * SW]
                    dve.wait_ge(glu_sig, k + 1)
                    nc.vector.tensor_tensor(sg[:, :, :], sg[:, :, :], ple[:, :, k * SW:(k + 1) * SW], ALU.mult).then_inc(glu_mul, 1)
                    dve.wait_ge(glu_mul, k + 1)
                    nc.vector.tensor_tensor(xs, xs, sg[:, :, :], ALU.add).then_inc(glu_sum, 1)
            dve.wait_ge(rms_sum, 4 + TT * DS)
            nc.vector.tensor_reduce(stat[:, 0, 0:2], stat[:, 2:4, 0:DS], AXX, ALU.add).then_inc(rms_mean, 1)
            dve.wait_ge(rms_mean, 3)
            nc.vector.tensor_scalar(stat[:, 0, 2:4], stat[:, 0, 0:2], 1.0 / D, EPS, ALU.mult, ALU.add).then_inc(rms_mean, 1)
            dve.wait_ge(rms_mean, 4)
            nc.vector.reciprocal(stat[:, 2, 4:6], stat[:, 0, 2:4]).then_inc(rms_inv, 1)
            dve.wait_ge(gfin_in, 16)
            dve.wait_ge(rms_ready, 3)
            for t, c in ((0, 0), (0, 1), (1, 1)):
                xs = x_res[:, t, c * HW:(c + 1) * HW]
                nc.vector.scalar_tensor_tensor(out=xs, in0=xs, scalar=stat[:, 2, 6 + t:7 + t], in1=g_fin_b[:, c * HW:(c + 1) * HW],
                                               op0=ALU.mult, op1=ALU.mult).then_inc(fin_ready[1], 1)

        @block.tensor
        def _(pe):
            def unit(n, us, g, par, hi, lo, kt, first, last):
                pe.wait_ge(lo_done, n + 1)
                if first and g is not None:
                    pe.wait_ge(free0, g - 1)
                    pe.wait_ge(free1, g - 1)
                for kk in range(UK):
                    for t in range(TT):
                        a = (kt + kk) * T + t * P
                        terms = ((hi, w_hi), (hi, w_lo), (lo, w_hi))
                        for s, (act_part, w_part) in enumerate(terms):
                            ins = nc.tensor.matmul(acc[:, 2 * par + t, :], act_part[:, a:a + P], w_part[:, us % SPL, kk, :],
                                                   start=first and kk == 0 and s == 0,
                                                   stop=last and kk == UK - 1 and s == 2)
                ins.then_inc(units_used, 1)

            def turn(r, b, src, kt, ready=None):
                if ready is not None:
                    pe.wait_ge(tr_lo, ready)
                for kk in range(2):
                    for t in range(TT):
                        ins = nc.tensor.transpose(side[:, b, kk * T + t * P:kk * T + (t + 1) * P],
                                                  src(t, kt + kk), ident[:, :])
                ins.then_inc(tr_full, 1)

            def turn_static(r, src, kt):
                turn(r, r % 4, src, kt, r - 3 if r >= 4 else None)

            def cols(tl):
                return lambda t, kt: tl[:, t, kt * P:(kt + 1) * P]

            pe.wait_ge(ident_in, 16)
            pe.wait_ge(g_in, 64)
            nc.tensor.transpose(acc[:, 3, 0:P], g_rows[:, :], ident[:, :]).then_inc(g_turned, 1)
            pe.wait_ge(x_half[0], 16)
            for r in range(4):
                turn_static(r, cols(x_in), 2 * r)
            pe.wait_ge(x_half[1], 16)
            for u in range(PAIR):
                if u < 8:
                    pe.wait_ge(tr_lo, u + 1)
                unit(u, u, None, u // UPS, a_hi, a_lo, u % UPS * UK, u % UPS == 0, u % UPS == UPS - 1)
                if u < 4:
                    turn_static(4 + u, cols(x_in), 8 + 2 * u)
            with pe.Fori(1, 3) as i:
                for u in range(PAIR):
                    j = u // UPS
                    unit(i * PAIR + u, u, i * 2 + j, j, a_hi, a_lo, u % UPS * UK, u % UPS == 0, u % UPS == UPS - 1)

            pe.wait_ge(preset, 1)
            pe.wait_ge(tables_in, 32)
            with pe.Fori(0, 4) as i:
                for j in range(2):
                    h = i * 2 + j
                    st = stage[j]
                    pe.wait_ge(sb_staged, h + 1)
                    for kind in range(2):
                        for t in range(TT):
                            ins = nc.tensor.transpose(side[:, 0, kind * T + t * P:kind * T + (t + 1) * P],
                                                      st[:, t, kind, :], ident[:, :])
                    ins.then_inc(sb_turned, 1)
                    for u in range(UPS):
                        v = U_HGP + j * UPS + u
                        unit(i * PAIR + v, v, i * 2 + (G_HGP + j), j, a_hi, a_lo, u * UK, u == 0, u == UPS - 1)
                        if u == 0:
                            pe.wait_ge(sb_q, h + 1)
                            pe.wait_ge(sb_k, h + 1)
                            nc.tensor.matmul(side[:, 1, 0:T], sb_kT[:, 0:P], sb_qT[:, :], start=True, stop=False,
                                             skip_group_check=True)
                            nc.tensor.matmul(side[:, 1, T:T + P], sb_kT[:, P:T], sb_qT[:, P:T], start=False, stop=False,
                                             skip_group_check=True).then_inc(sb_z, 1)
                        if u == 2:
                            pe.wait_ge(sb_masked, h + 1)
                            nc.tensor.matmul(side[:, 1, 0:T], ntri[:, :], sp[:, 0:T], start=False, stop=False,
                                             skip_group_check=True)
                            nc.tensor.matmul(side[:, 1, P:T], nones[:, :], sp[:, T:T + P], start=False, stop=False,
                                             skip_group_check=True)
                            nc.tensor.matmul(side[:, 1, T:T + P], ntri[:, :], sp[:, T:T + P], start=False, stop=True,
                                             skip_group_check=True).then_inc(sb_later, 1)
                        if u == 4:
                            pe.wait_ge(sb_wm, h + 1)
                            nc.tensor.matmul(side[:, 3, 0:T], st[:, 0, 2, :], wt[:, 0:T], start=True, stop=False)
                            nc.tensor.matmul(side[:, 3, P:T], st[:, 1, 2, :], wt[:, T:T + P], start=False,
                                             stop=True).then_inc(sb_o, 1)

            pe.wait_ge(preset, 3)
            with pe.Fori(0, 4) as i:
                for j in range(2):
                    h = i * 2 + j
                    v0, g0 = h * V_STEPS, h * G_STEPS
                    pe.wait_ge(hg_prep, h * 2 + 1)
                    for t in range(TT):
                        nc.tensor.transpose(side[:, 0, t * P:(t + 1) * P], s_f[:, t, :], ident[:, :])
                        ins = nc.tensor.transpose(side[:, 0, T + t * P:T + (t + 1) * P], st_q[:, t, :], ident[:, :])
                    ins.then_inc(hg_turned, 1)

                    def level(n, bank, pos):
                        q, k = (q_dia[:, :], k_lev[:, 0, :]) if n == 0 else (q_lev[:, n - 1, :], k_lev[:, n - 1, :])
                        for t in range(TT):
                            ins = nc.tensor.matmul(side[:, bank, pos * T + t * P:pos * T + (t + 1) * P],
                                                   k[:, t * P:(t + 1) * P], q[:, t * P:(t + 1) * P], start=True, stop=True)
                        return ins

                    for u in range(UPS):
                        v = U_GAT + j * UPS + u
                        unit(i * PAIR + v, v, i * 2 + (G_GAT + j), j, a_hi, a_lo, u * UK, u == 0, u == UPS - 1)
                        if u == 2:
                            pe.wait_ge(hg_q, h + 1)
                            pe.wait_ge(hg_vec, v0 + v_q(2))
                            pe.wait_ge(hg_key, g0 + 4)
                            for n in range(4):
                                ins = level(n, 1 + n // 2, n % 2)
                            ins.then_inc(hg_s1, 1)
                        if u == 4:
                            pe.wait_ge(hg_vec, v0 + v_s(4))
                            pe.wait_ge(hg_key, g0 + G_STEPS)
                            for n in range(4, 8):
                                level(n, (3, 0)[(n - 4) // 2], n % 2)
                            nc.tensor.matmul(side[:, 1, 0:P], k_lev[:, 7, 0:P], q_lev[:, 7, P:T], start=True,
                                             stop=True).then_inc(hg_s2, 1)
                        if u == 6:
                            pe.wait_ge(hg_vec, v0 + v_s(8))
                            pe.wait_ge(hg_cross, h + 1)
                            vh = [hgp_v[:, 1, t, ds(h * P, P)] for t in range(TT)]
                            nc.tensor.matmul(side[:, 2, 0:P], score[:, 0:P], vh[0], start=True, stop=True)
                            nc.tensor.matmul(side[:, 2, P:T], cross[:, :], vh[0], start=True, stop=False)
                            nc.tensor.matmul(side[:, 2, P:T], score[:, P:T], vh[1], start=False, stop=True).then_inc(hg_o, 1)

            pe.wait_ge(hg_out, HEADS)
            pe.wait_ge(sb_lo, HEADS)
            hgy_v = hgy.rearrange("p (t c) -> p t c", t=TT)
            for u in range(PAIR):
                unit(U_WSB + u, U_WSB + u, G_WSB + u // 4, u // 4 % 2, b_hi, b_lo, u % 4 * UK, u % 4 == 0, u % 4 == 3)
                if 9 <= u < 13:
                    pe.wait_ge(hn_y, 1)
                    turn_static(R_HG + u - 9, cols(hgy_v), 2 * (u - 9))

            def y_cols(t, kt):
                return gate(0, kt // 4)[:, t, kt % 4 * P:(kt % 4 + 1) * P]

            for u in range(PAIR):
                if u < 4:
                    pe.wait_ge(tr_lo, R_HG + u + 1)
                unit(U_WHG + u, U_WHG + u, G_WHG + u // 4, u // 4 % 2, b_hi, b_lo, HEADS + u % 4 * UK, u % 4 == 0, u % 4 == 3)
                if u in (6, 10, 14):
                    k = (u - 6) // 4
                    pe.wait_ge(y_ready, k + 1)
                    for b in range(2):
                        turn_static(R_Y + 2 * k + b, y_cols, 4 * k + 2 * b)
            for u in range(DS * UPS):
                if u < UPS:
                    pe.wait_ge(tr_lo, R_Y + u + 1)
                unit(U_OUT + u, U_OUT + u, G_OUT + u // UPS, u // UPS % 2, a_hi, a_lo, u % UPS * UK, u % UPS == 0,
                     u % UPS == UPS - 1)
                if u == 2:
                    pe.wait_ge(y_ready, 4)
                    for b in range(2):
                        turn_static(R_Y + 6 + b, y_cols, 12 + 2 * b)
                if u in (10, 18, 26):
                    k = (u - 10) // 8
                    pe.wait_ge(free1, G_OUT + k + 1)
                    for b in range(2):
                        turn_static(R_X1 + 2 * k + b, cols(x_res), 4 * k + 2 * b)
                if u == 28:
                    pe.wait_ge(p_in_s, 16)
                    turn_static(R_P, cols(p_in), 0)
            for u in range(DS):
                if u == 0:
                    pe.wait_ge(tr_lo, R_P + 1)
                unit(U_PLE + u, U_PLE + u, G_PLE + u, u % 2, u_hi, u_lo, 0, True, True)
                if u == 1:
                    pe.wait_ge(free1, G_OUT + 4)
                    for b in range(2):
                        turn_static(R_X1B + b, cols(x_res), 12 + 2 * b)
            with pe.Fori(0, QUARTERS) as q:
                for u in range(QU):
                    v, k = U_MLP + u, u // UPS
                    if k == 0:
                        pe.wait_ge(tr_lo, R_U)
                    if k == DS:
                        pe.wait_ge(tr_lo, q * 8 + (R_U + u % UPS + 1))
                    hi, lo = (b_hi, b_lo) if k < DS else (u_hi, u_lo)
                    unit(q * QU + v, v, q * 2 * DS + (G_MLP + k), k % 2, hi, lo, u % UPS * UK, u % UPS == 0, u % UPS == UPS - 1)
                    if u % UPS == 2 and UPS < u < DS * UPS + UPS:
                        k -= 1
                        pe.wait_ge(usq_done, q * DS + (k + 1))
                        for b in range(2):
                            r = R_U + 2 * k + b
                            turn(r, r % 4, lambda t, kt: usq[:, t, kt * P:(kt + 1) * P], 2 * b, q * 8 + (r - 3))
            for b in range(4):
                turn_static(R_X2 + b, cols(x_res), 2 * b)
            for u in range(DS * UPS):
                if u < UPS:
                    pe.wait_ge(tr_lo, R_X2 + u + 1)
                if u // UPS >= 2 and u % UPS == 0:
                    pe.wait_ge(glu_sig, u // UPS - 1)
                unit(U_GLU + u, U_GLU + u, G_GLU + u // UPS if u // UPS < 2 else None, u // UPS % 2, a_hi, a_lo,
                     u % UPS * UK, u % UPS == 0, u % UPS == UPS - 1)
                if u < 4:
                    if u == 2:
                        pe.wait_ge(free1, G_GLU)
                    turn_static(R_X2 + 4 + u, cols(x_res), 8 + 2 * u)


def kernel(x, p, mix_norm_g, w_in, hgrn_lb_logits, hgrn_out_norm_g, w_o_sb, w_o_hg, w_out, mlp_norm_g, w_up, w_down,
           w_ple_proj, w_ple_gate, final_norm_g):
    import concourse.bacc as bacc
    from concourse.bass_utils import run_bass_kernel_spmd

    row = np.arange(P)
    key, query = row[:, None], row[None, :]
    levels = [key == query]
    for j in range(LEVELS - 1):
        m = 1 << j
        levels.append((query // m % 2 == 1) & (key // m == query // m - 1))
    masks = np.concatenate([np.tile(lv, (1, TT)) for lv in levels], axis=1).astype(np.float32)
    arrays = {
        "x": x[0], "p": p[0, 0], "g_mix": mix_norm_g, "w_in": w_in[0], "lb_logits": hgrn_lb_logits,
        "g_hg": hgrn_out_norm_g, "w_o_sb": w_o_sb[0], "w_o_hg": w_o_hg[0], "w_out": w_out[0], "g_mlp": mlp_norm_g,
        "w_up": w_up[0], "w_down": w_down[0], "w_ple": w_ple_proj[0], "w_glu": w_ple_gate[0], "g_fin": final_norm_g,
        "c_ident": np.eye(P, dtype=np.float32), "c_ntri": -(key >= query).astype(np.float32), "c_masks": masks,
    }
    nc = bacc.Bacc("TRN2", target_bir_lowering=False, num_devices=1)
    maps, args = {}, []
    for name, a in arrays.items():
        a = np.ascontiguousarray(a)
        maps[f"in_{name}"] = a
        args.append(nc.dram_tensor(f"in_{name}", a.shape, mybir.dt.from_np(a.dtype), kind="ExternalInput").ap())
    args.append(nc.dram_tensor("out_0", (T, D), F32, kind="ExternalOutput").ap())
    build(nc, *args)
    result = run_bass_kernel_spmd(nc, [maps], core_ids=[0])
    return result.results[0]["out_0"].reshape(x.shape)
```

```python
from contextlib import ExitStack

import numpy as np

import concourse.bass as bass
from concourse import mybir

F32 = mybir.dt.float32
F32R = mybir.dt.float32r
U8 = mybir.dt.uint8
ACT = mybir.ActivationFunctionType
ALU = mybir.AluOpType
AXX = mybir.AxisListType.X
ds = bass.ds

P = 128
D = 2048
T = 256
TT = T // P
HEADS = 8
HW = HEADS * P
FF = 4 * D
PLE = 256
EPS = 1e-6
SW = 512
KT = D // P
UK = 2
UPS = KT // UK
PAIR = 2 * UPS
RAW = 8
SPL = 4
LEAD = 3
DS = D // SW
G_COLS = 2 * KT + 3 * HEADS
X_CUTS = (0, SW // 2, SW, 2 * SW, 3 * SW, D)
QUARTERS = 4
LEVELS = 8

U_QKV, G_QKV = 0, 0
U_HGP, G_HGP = U_QKV + 3 * PAIR, G_QKV + 6
U_GAT, G_GAT = U_HGP + 4 * PAIR, G_HGP + 8
U_WSB, G_WSB = U_GAT + 4 * PAIR, G_GAT + 8
U_WHG, G_WHG = U_WSB + PAIR, G_WSB + DS
U_OUT, G_OUT = U_WHG + PAIR, G_WHG + DS
U_PLE, G_PLE = U_OUT + DS * UPS, G_OUT + DS
U_MLP, G_MLP = U_PLE + DS, G_PLE + DS
QU = 2 * DS * UPS
U_GLU, G_GLU = U_MLP + QUARTERS * QU, G_MLP + QUARTERS * 2 * DS
U_END = U_GLU + DS * UPS

R_X = 0
R_HG = R_X + 8
R_Y = R_HG + 4
R_X1 = R_Y + 8
R_P = R_X1 + 6
R_X1B = R_P + 1
R_U = R_X1B + 2
R_X2 = R_U + QUARTERS * 8

V_F, V_K0, V_Q0 = 1, 2, 3
V_STEPS = 31


def v_t(j):
    return V_F if j == 0 else 3 * j + 1


def v_q(j):
    return V_Q0 if j == 0 else (3 * j + 3 if j < 7 else 23)


def v_s(n):
    return 23 + n


G_STEPS = 14


def build(nc, x, p, g_mix, w_in, lb_logits, g_hg, w_o_sb, w_o_hg, w_out, g_mlp, w_up, w_down,
          w_ple, w_glu, g_fin, c_ident, c_ntri, c_masks, out):
    ctx = ExitStack()
    with ctx:
        def sem(name):
            return ctx.enter_context(nc.semaphore(name))

        at = [(nc.sbuf_base + 63) // 64 * 64]

        def take(n):
            at[0] += n
            return at[0] - n

        def tile(name, shape, dt, offset):
            return nc.alloc_sbuf_tensor_at(name, shape, dt, offset=offset)

        KB = 1024
        raw = tile("raw", [P, RAW, UK, SW], F32, take(32 * KB))
        w_hi = tile("w_hi", [P, SPL, UK, SW], F32R, take(16 * KB))
        w_lo = tile("w_lo", [P, SPL, UK, SW], F32R, take(16 * KB))
        a_hi = tile("a_hi", [P, KT * T], F32R, take(16 * KB))
        a_lo = tile("a_lo", [P, KT * T], F32R, take(16 * KB))
        at_b = take(32 * KB)
        b_hi = tile("b_hi", [P, KT * T], F32R, at_b)
        b_lo = tile("b_lo", [P, KT * T], F32R, at_b + 16 * KB)
        q_lev = tile("q_lev", [P, 8, T], F32, at_b + 8 * KB)
        k_lev = tile("k_lev", [P, 8, T], F32, at_b + 24 * KB)
        masks_in = tile("masks_in", [P, T + 7 * P], F32, at_b + 24 * KB)
        at_1 = take(32 * KB)
        qkv = tile("qkv", [P, TT * 3 * HW], F32, at_1)
        stage = [tile(f"stage{j}", [P, TT, 3, P], F32, at_1 + (24 + 3 * j) * KB) for j in range(2)]
        sb_qT = tile("sb_qT", [P, T], F32, at_1 + 30 * KB)
        sb_kT = tile("sb_kT", [P, T], F32, at_1 + 31 * KB)
        square = tile("square", [P, D], F32, at_1)
        gates = tile("gates", [P, 4 * TT * HW], F32, at_1)
        u_hi = tile("u_hi", [P, KT * T], F32R, at_1)
        u_lo = tile("u_lo", [P, KT * T], F32R, at_1 + 16 * KB)
        square1 = tile("square1", [P, D], F32, at_1 + 8 * KB)
        g_fin_b = tile("g_fin_b", [P, D], F32, at_1)
        square2 = tile("square2", [P, SW], F32, at_1 + 8 * KB)
        at_2 = take(32 * KB)
        x_in = tile("x_in", [P, TT, D], F32, at_2)
        hgp = tile("hgp", [P, 4 * TT * HW], F32, at_2)
        x_res = tile("x_res", [P, TT, D], F32, at_2)
        ple = tile("ple", [P, TT, D], F32, at_2 + 16 * KB)
        ident = tile("ident", [P, P], F32, take(512))
        ntri = tile("ntri", [P, P], F32, take(512))
        nones = tile("nones", [P, P], F32, take(512))
        masks = tile("masks", [P, T + 7 * P], U8, take(T + 7 * P))
        g_first = tile("g_first", [P, P], F32, take(512))
        g_rows = tile("g_rows", [P, P], F32, take(512))
        gT = tile("gT", [P, G_COLS], F32, take(256))
        lb2 = tile("lb2", [P, 2, HEADS], F32, take(64))
        lb_s = tile("lb_s", [P, 4, HEADS], F32, take(128))
        lbT = tile("lbT", [P, 2, HEADS], F32, take(64))
        lb_h = tile("lb_h", [P, 2, 1], F32, take(32))
        stat = tile("stat", [P, 4, 8], F32, take(128))
        stat_h = tile("stat_h", [P, 3, 16], F32, take(192))
        at_s = take(0)
        sp = tile("sp", [P, 3 * P], F32, at_s)
        wt = tile("wt", [P, 3 * P], F32, at_s + 1536)
        s_f = tile("s_f", [P, TT, P], F32, at_s)
        s_qg = tile("s_qg", [P, 2, TT, P], F32, at_s + 1 * KB)
        st_q = tile("st_q", [P, TT, P], F32, at_s + 3 * KB)
        q_dia = tile("q_dia", [P, T], F32, at_s + 4 * KB)
        t_lev = [tile(f"t_lev{j}", [P, T >> j], F32, at_s + 5 * KB + (2 * KB - (2 * KB >> j))) for j in range(7)]
        score = tile("score", [P, T], F32, at_s + 7 * KB)
        cross = tile("cross", [P, P], F32, at_s + 8 * KB)
        un = tile("un", [P, TT, SW], F32, at_s)
        usq = tile("usq", [P, TT, SW], F32, at_s + 4 * KB)
        p_in = tile("p_in", [P, TT, PLE], F32, at_s)
        assert at_s + 8 * KB + 512 <= nc.sbuf_usable_end

        acc = ctx.enter_context(nc.psum_tensor("acc", [P, 4, SW], F32))
        side = ctx.enter_context(nc.psum_tensor("side", [P, 4, SW], F32))

        raw_full = [sem(f"raw_full{s}") for s in range(RAW)]
        hi_done = sem("hi_done")
        lo_done = sem("lo_done")
        units_used = sem("units_used")
        free0 = sem("free0")
        free1 = sem("free1")
        tr_full = sem("tr_full")
        tr_hi = sem("tr_hi")
        tr_lo = sem("tr_lo")
        ident_in, x_piece, tables_in = sem("ident_in"), [sem(f"x_piece{c}") for c in range(len(X_CUTS) - 1)], sem("tables_in")
        g_zero, g_in, g_turned, g_ready = sem("g_zero"), sem("g_in"), sem("g_turned"), sem("g_ready")
        xres_in, p_in_s, gfin_in, stored = sem("xres_in"), sem("p_in_s"), sem("gfin_in"), sem("stored")
        preset = sem("preset")
        g_first_in = sem("g_first_in")
        rms_sum, rms_inv, rms_ready = sem("rms_sum"), sem("rms_inv"), sem("rms_ready")
        rms_mean = sem("rms_mean")
        lb_vec, lb_exp = sem("lb_vec"), sem("lb_exp")
        sb_staged, sb_turned, sb_q, sb_k = sem("sb_staged"), sem("sb_turned"), sem("sb_q"), sem("sb_k")
        sb_z, sb_soft, sb_keep, sb_masked = sem("sb_z"), sem("sb_soft"), sem("sb_keep"), sem("sb_masked")
        sb_later, sb_w, sb_wm = sem("sb_later"), sem("sb_w"), sem("sb_wm")
        sb_o, sb_hi, sb_lo = sem("sb_o"), sem("sb_hi"), sem("sb_lo")
        hg_sig, hg_prep, hg_turned, hg_q = sem("hg_sig"), sem("hg_prep"), sem("hg_turned"), sem("hg_q")
        hg_vec, hg_key, hg_s1, hg_s2 = sem("hg_vec"), sem("hg_key"), sem("hg_s1"), sem("hg_s2")
        hg_cross, hg_o, hg_out = sem("hg_cross"), sem("hg_o"), sem("hg_out")
        hn_sq, hn_mean, hn_inv, hn_rstd, hn_mul, hn_y = (sem("hn_sq"), sem("hn_mean"), sem("hn_inv"),
                                                         sem("hn_rstd"), sem("hn_mul"), sem("hn_y"))
        y_ready, usq_done = sem("y_ready"), sem("usq_done")
        glu_sig, glu_mul, glu_sum = sem("glu_sig"), sem("glu_mul"), sem("glu_sum")
        fin_first, fin_gain = sem("fin_first"), sem("fin_gain")
        fin_vec, fin_pool, fin_act = sem("fin_vec"), sem("fin_pool"), sem("fin_act")

        qkv_v = qkv[:, :].rearrange("p (t k c) -> p t k c", t=TT, k=3)
        hgp_v = hgp[:, :].rearrange("p (k t c) -> p k t c", k=4, t=TT)
        hgf = hgp[:, 0:TT * HW]
        hgo = hgp[:, TT * HW:2 * TT * HW]
        hgy = hgp[:, 2 * TT * HW:3 * TT * HW]
        hgg = hgp[:, 3 * TT * HW:4 * TT * HW]

        def gate(kind, k):
            return gates[:, :].rearrange("p (i t c) -> p i t c", i=4, t=TT)[:, 2 * kind + k // 2, :,
                                                                           k % 2 * SW:k % 2 * SW + SW]

        def even_odd(row, m):
            v = row.rearrange("p (b two m) -> p b two m", two=2, m=m)
            return v[:, :, 0, :], v[:, :, 1, :]

        def totals(j):
            n = T >> (j + 1)
            v = t_lev[j][:, :].rearrange("p (b two) -> p b two", two=2)
            return (v[:, :, 0:1].to_broadcast([P, n, 1 << j]), v[:, :, 1:2].to_broadcast([P, n, 1 << j]))

        def score_place(n):
            if n < 3:
                return 1, (0, T, T + P)[n]
            return (2, 0) if n == 3 else (3, (n - 4) * P)

        def upper(t):
            return t[:, :].rearrange("p (b c) -> p b c", b=3)[:, 0:3:2, :]

        block = ctx.enter_context(nc.Block())

        @block.sync
        def _(spe):
            def load(n, us, src):
                if us >= RAW:
                    spe.wait_ge(lo_done, n - (RAW - 1))
                spe.dma_start(raw[:, us % RAW, :, :], src).then_inc(raw_full[us % RAW], 16)

            def part(w, row, col):
                return w[ds(row, UK * P), ds(col, SW)].rearrange("(k q) n -> q k n", q=P)

            def in_unit(i, u, us):
                load(i * PAIR + u, us, part(w_in, u % UPS * UK * P, i * 2 * SW + u // UPS * SW))

            spe.dma_start(ident[:, :], c_ident).then_inc(ident_in, 16)
            xv = x.rearrange("(t p) n -> p t n", p=P)
            for u in range(PAIR):
                if u * UK * P in X_CUTS[:-1]:
                    c = X_CUTS.index(u * UK * P)
                    cols = slice(X_CUTS[c], X_CUTS[c + 1])
                    spe.dma_start(x_in[:, :, cols], xv[:, :, cols]).then_inc(x_piece[c], 16)
                in_unit(0, u, u)
            with spe.Fori(1, 11) as i:
                for u in range(PAIR):
                    in_unit(i, u, u + RAW)
            for w, base in ((w_o_sb, U_WSB), (w_o_hg, U_WHG)):
                for u in range(PAIR):
                    load(base + u, base + u, part(w, u % 4 * UK * P, u // 4 * SW))
            spe.wait_ge(hn_y, 1)
            spe.wait_ge(tr_lo, R_Y)
            spe.dma_start(x_res[:, :, :], xv).then_inc(xres_in, 16)
            spe.dma_start(p_in[:, :, :], p.rearrange("(t p) n -> p t n", p=P)).then_inc(p_in_s, 16)
            for u in range(DS * UPS):
                load(U_OUT + u, U_OUT + u, part(w_out, u % UPS * UK * P, u // UPS * SW))
            for u in range(DS):
                load(U_PLE + u, U_PLE + u, part(w_ple, 0, u * SW))
            with spe.Fori(0, QUARTERS) as q:
                for u in range(DS * UPS):
                    load(q * QU + (U_MLP + u), U_MLP + u, part(w_up, u % UPS * UK * P, q * D + u // UPS * SW))
                for u in range(DS * UPS):
                    v = DS * UPS + u
                    load(q * QU + (U_MLP + v), U_MLP + v, part(w_down, q * D + u % UPS * UK * P, u // UPS * SW))
            for u in range(DS * UPS):
                if u == 12:
                    spe.wait_ge(units_used, U_GLU)
                    spe.dma_start(g_fin_b[:, :], g_fin.partition_broadcast(P)).then_inc(gfin_in, 16)
                load(U_GLU + u, U_GLU + u, part(w_glu, u % UPS * UK * P, u // UPS * SW))
            ov = out.rearrange("(t p) n -> p t n", p=P)
            for t in range(TT):
                for k, tl, scaled, n in ((3, x_res, fin_vec, 2 * t + 1), (0, ple, (fin_pool, fin_act)[t], 1),
                                         (2, ple, fin_vec, 2 * t + 2), (1, ple, (fin_pool, fin_act)[t], 2)):
                    spe.wait_ge(scaled, n)
                    spe.dma_start(ov[:, t, k * SW:(k + 1) * SW], tl[:, t, k * SW:(k + 1) * SW]).then_inc(stored, 16)
            spe.wait_ge(stored, TT * DS * 16)

        @block.gpsimd
        def _(pool):
            nc.gpsimd.memset(g_first[:, :], 0.0).then_inc(g_zero, 1)
            nc.gpsimd.memset(g_rows[:, :], 0.0).then_inc(g_zero, 1)
            nc.gpsimd.memset(nones[:, :], -1.0).then_inc(preset, 1)

            pool.wait_ge(tables_in, 32)
            nc.gpsimd.tensor_copy(masks[:, :], masks_in[:, :]).then_inc(preset, 1)

            def staged(h, i, j):
                pool.wait_ge(free0, i + 5)
                pool.wait_ge(free1, i + 5)
                pool.wait_ge(units_used, (h + 5) * UPS)
                nc.gpsimd.tensor_copy(stage[j][:, :, :, :], qkv_v[:, :, :, ds(h * P, P)]).then_inc(sb_staged, 1)

            def keep_earlier(tl):
                pool.nop(nofuse=True)
                return nc.gpsimd.affine_select(out=upper(tl), in_=upper(tl), compare_op=ALU.is_gt, fill=0.0,
                                               base=0, pattern=[[0, 2], [1, P]], channel_multiplier=-1)

            with pool.Fori(0, 4) as i:
                for j in range(2):
                    h = i * 2 + j
                    staged(h, i, j)
                    pool.wait_ge(sb_keep, h + 1)
                    keep_earlier(sp).then_inc(sb_masked, 1)
                    pool.wait_ge(sb_w, h + 1)
                    keep_earlier(wt).then_inc(sb_wm, 1)

            pool.wait_ge(sb_o, HEADS)
            pool.wait_ge(lb_vec, 6)
            nc.gpsimd.memset(score[:, :], 0.0).then_inc(preset, 1)
            with pool.Fori(0, 4) as i:
                for j in range(2):
                    h = i * 2 + j
                    pool.wait_ge(hg_sig, h + 1)
                    nc.gpsimd.tensor_copy(lb_h[:, :, :], lbT[:, :, ds(h, 1)])
                    nc.gpsimd.tensor_tensor(st_q[:, :, :], s_qg[:, 0, :, :], hgp_v[:, 2, :, ds(h * P, P)],
                                            ALU.mult).then_inc(hg_prep, 1)
                    nc.gpsimd.tensor_tensor(hgp_v[:, 3, :, ds(h * P, P)], s_qg[:, 1, :, :],
                                            hgp_v[:, 3, :, ds(h * P, P)], ALU.mult).then_inc(hg_prep, 1)
                    for lev in range(7):
                        pool.wait_ge(hg_vec, h * V_STEPS + max(v_t(lev), V_K0 if lev == 0 else 0))
                        if lev:
                            pool.wait_ge(hg_key, h * G_STEPS + 2 * lev)
                        src, dst = (even_odd(k_lev[:, lv, :], 1 << lev) for lv in (lev, lev + 1))
                        nc.gpsimd.tensor_tensor(dst[0], src[0], totals(lev)[1], ALU.mult).then_inc(hg_key, 1)
                        nc.gpsimd.tensor_copy(dst[1], src[1]).then_inc(hg_key, 1)

            pool.wait_ge(hn_mul, 1)
            nc.gpsimd.tensor_tensor(hgy, hgy, hgg, ALU.mult).then_inc(hn_y, 1)
            for k in range(DS):
                pool.wait_ge(free1, G_WHG + k + 1)
                nc.gpsimd.tensor_tensor(gate(0, k), gate(0, k), gate(1, k), ALU.add).then_inc(y_ready, 1)
            with pool.Fori(0, QUARTERS) as q:
                for k in range(DS):
                    pool.wait_ge(free1, q * 2 * DS + (G_MLP + k + 1))
                    pool.wait_ge(tr_full, q * 8 + (R_U + 2 * k))
                    nc.gpsimd.tensor_tensor(usq[:, :, :], un[:, :, :], un[:, :, :], ALU.mult).then_inc(usq_done, 1)
            pool.wait_ge(gfin_in, 16)
            for k in range(DS - 1):
                pool.wait_ge(glu_sum, k + 1)
                for t in range(TT):
                    strip = slice(k * SW, (k + 1) * SW)
                    nc.gpsimd.tensor_tensor(ple[:, t, strip], x_res[:, t, strip], g_fin_b[:, strip],
                                            ALU.mult).then_inc(fin_gain, 1)
            pool.wait_ge(fin_gain, TT * (DS - 1))
            pool.wait_ge(rms_ready, 3)
            for k in range(2):
                strip = slice(k * SW, (k + 1) * SW)
                nc.gpsimd.tensor_scalar(ple[:, 0, strip], ple[:, 0, strip], stat[:, 2, 6:7], None,
                                        ALU.mult).then_inc(fin_pool, 1)

        @block.scalar
        def _(act):
            def split(us, i=0, step=0):
                act.wait_ge(raw_full[us % RAW], i * (16 * step // RAW) + 16 * (us // RAW + 1))
                if us >= SPL or step:
                    act.wait_ge(units_used, i * step + (us - SPL + 1))
                nc.scalar.activation(w_hi[:, us % SPL, :, :], raw[:, us % RAW, :, :], ACT.Copy).then_inc(hi_done, 1)

            def evac(dst, used, par, t, func, **kw):
                act.wait_ge(units_used, used)
                nc.scalar.activation(dst, acc[:, 2 * par + t, :], func, **kw).then_inc((free0, free1)[t], 1)

            def turned(r, dst, col=None, kt=0):
                act.wait_ge(tr_full, r + 1)
                b = r % 4
                if col is None:
                    nc.scalar.activation(dst[:, kt * T:(kt + 2) * T], side[:, b, :], ACT.Copy).then_inc(tr_hi, 1)
                    return
                for kk in range(2):
                    ins = nc.scalar.activation(dst[:, (kt + kk) * T:(kt + kk + 1) * T], side[:, b, kk * T:(kk + 1) * T],
                                               ACT.Copy, scale=gT[:, col + kt + kk:col + kt + kk + 1])
                ins.then_inc(tr_hi, 1)

            def rows_in(tl, row, k, g, landed):
                act.dma_start(tl[row:row + k, :], g.rearrange("a (k p) -> (a k) p", p=P)).then_inc(landed, 16)

            act.wait_ge(g_zero, 1)
            rows_in(g_first, 0, KT, g_mix, g_first_in)
            act.wait_ge(preset, 1)
            nc.scalar.activation(stat[:, 3, 4:5], nones[:, 0:1], ACT.Copy)
            act.wait_ge(g_ready, 1)
            turned(0, a_hi, 0, 0)
            split(0)
            turned(1, a_hi, 0, 2)
            split(1)
            split(2)

            def qkv_evac(i, j):
                evac(qkv[:, ds(i * HW + j * SW, SW)], i * PAIR + (j + 1) * UPS, j, 0,
                     ACT.Copy, scale=stat[:, 0, 6:7])

            for u in range(PAIR):
                split(u + LEAD)
                if u < 6:
                    turned(2 + u, a_hi, 0, 4 + 2 * u)
                if u == 2:
                    act.wait_ge(g_zero, 2)
                    for row, k, g in ((0, KT, g_mlp), (KT, HEADS, g_hg), (KT + HEADS, 2 * HEADS, lb_logits)):
                        rows_in(g_rows, row, k, g, g_in)
                if u == 6:
                    for t in range(TT):
                        ins = nc.scalar.activation(square[:, :], x_in[:, t, :], ACT.Square, accum_out=stat[:, 0, t:t + 1])
                        ins.then_inc(rms_sum, 1)
                        act.wait_ge(rms_sum, t + 1)
                    act.wait_ge(rms_inv, 1)
                    nc.scalar.activation(stat[:, 0, 6:8], stat[:, 0, 4:6], ACT.Sqrt).then_inc(rms_ready, 1)
                    act.wait_ge(rms_ready, 1)
                if u == 8:
                    act.dma_start(ntri[:, :], c_ntri).then_inc(tables_in, 16)
                    act.dma_start(masks_in[:, :], c_masks).then_inc(tables_in, 16)
                    act.wait_ge(lb_vec, 2)
                    nc.scalar.activation(lb_s[:, 0:2, :], lb2[:, :, :], ACT.Exp).then_inc(lb_exp, 1)
                if u % UPS == UPS - 1:
                    qkv_evac(0, u // UPS)
            with act.Fori(1, 3) as i:
                for u in range(PAIR):
                    split(u + LEAD, i, PAIR)
                    if u % UPS == UPS - 1:
                        qkv_evac(i, u // UPS)

            with act.Fori(0, 4) as i:
                for j in range(2):
                    h = i * 2 + j
                    act.wait_ge(sb_turned, h + 1)
                    nc.scalar.activation(sb_qT[:, :], side[:, 0, 0:T], ACT.Copy, scale=float(P) ** -0.5).then_inc(sb_q, 1)
                    for u in range(UPS):
                        v = U_HGP + j * UPS + u
                        split(v + LEAD, i, PAIR)
                        if u == 0:
                            act.wait_ge(sb_z, h + 1)
                            nc.scalar.activation(sp[:, :], side[:, 1, 0:3 * P], ACT.Abs).then_inc(sb_soft, 1)
                            act.wait_ge(sb_soft, h * 3 + 1)
                            nc.scalar.activation(sp[:, :], sp[:, :], ACT.Exp, scale=-1.0).then_inc(sb_soft, 1)
                            act.wait_ge(sb_soft, h * 3 + 2)
                            nc.scalar.activation(sp[:, :], sp[:, :], ACT.Ln, bias=1.0).then_inc(sb_soft, 1)
                        if u == 2:
                            act.wait_ge(sb_later, h + 1)
                            nc.scalar.activation(wt[:, :], side[:, 1, 0:3 * P], ACT.Exp).then_inc(sb_w, 1)
                        if u == 4:
                            act.wait_ge(sb_o, h + 1)
                            nc.scalar.activation(b_hi[:, ds(h * T, T)], side[:, 3, 0:T], ACT.Copy).then_inc(sb_hi, 1)
                    evac(hgp[:, ds(i * TT * HW + j * SW, SW)], i * PAIR + (U_HGP + (j + 1) * UPS), j, 0,
                         ACT.Copy, scale=stat[:, 0, 6:7])

            with act.Fori(0, 4) as i:
                for j in range(2):
                    h = i * 2 + j
                    if j == 0:
                        act.wait_ge(free1, i + (G_GAT - 1))
                    nc.scalar.activation(s_f[:, :, :], hgp_v[:, 0, :, ds(h * P, P)], ACT.Sigmoid)
                    nc.scalar.activation(s_qg[:, :, :, :], hgp_v[:, 2:4, :, ds(h * P, P)], ACT.Sigmoid).then_inc(hg_sig, 1)
                    for u in range(UPS):
                        v = U_GAT + j * UPS + u
                        split(v + LEAD, i, PAIR)
                        if u == 1:
                            act.wait_ge(hg_turned, h + 1)
                            nc.scalar.activation(q_dia[:, :], side[:, 0, T:2 * T], ACT.Copy).then_inc(hg_q, 1)
                        if u == 5:
                            act.wait_ge(hg_s2, h + 1)
                            nc.scalar.activation(cross[:, :], side[:, 0, 0:P], ACT.Copy).then_inc(hg_cross, 1)
                    for t in range(TT):
                        evac(gates[:, ds(i * TT * HW + t * HW + j * SW, SW)], i * PAIR + (U_GAT + (j + 1) * UPS), j, t,
                             ACT.Sigmoid, scale=stat[:, 0, 6 + t:7 + t])
                    act.wait_ge(hg_o, h + 1)
                    nc.scalar.activation(hgp_v[:, 1, :, ds(h * P, P)], side[:, 2, 0:T].rearrange("p (t c) -> p t c", t=TT),
                                         ACT.Copy).then_inc(hg_out, 1)

            def splits(base, u):
                if base + u + LEAD < U_END:
                    split(base + u + LEAD)

            for u in range(PAIR):
                splits(U_WSB, u)
                if u == 0:
                    act.wait_ge(hg_out, HEADS)
                    nc.scalar.activation(hgf, hgo, ACT.Square).then_inc(hn_sq, 1)
                if u == 3:
                    act.wait_ge(hn_inv, 1)
                    nc.scalar.activation(stat_h[:, 2, :], stat_h[:, 1, :], ACT.Sqrt).then_inc(hn_rstd, 1)
                if 9 <= u < 13:
                    turned(R_HG + u - 9, b_hi, 2 * KT - HEADS, HEADS + 2 * (u - 9))
            for u in range(PAIR):
                splits(U_WHG, u)
                if u in (6, 10, 14):
                    k = (u - 6) // 4
                    for b in range(2):
                        turned(R_Y + 2 * k + b, a_hi, None, 4 * k + 2 * b)
            for u in range(DS * UPS):
                splits(U_OUT, u)
                if u == 2:
                    for b in range(2):
                        turned(R_Y + 6 + b, a_hi, None, 12 + 2 * b)
                if u in (10, 18, 26):
                    k = (u - 10) // 8
                    for b in range(2):
                        turned(R_X1 + 2 * k + b, b_hi, KT, 4 * k + 2 * b)
                if u == 28:
                    turned(R_P, u_hi)
            for u in range(DS):
                splits(U_PLE, u)
                if u == 1:
                    for b in range(2):
                        turned(R_X1B + b, b_hi, KT, 12 + 2 * b)
                evac(ple[:, 0, u * SW:(u + 1) * SW], U_PLE + u + 1, u % 2, 0, ACT.Copy)
                if u >= 2:
                    act.wait_ge(rms_sum, u)
                    nc.scalar.activation(square1[:, :], x_res[:, u - 2, :], ACT.Square,
                                         accum_out=stat[:, 1, u - 2:u - 1]).then_inc(rms_sum, 1)
            act.wait_ge(rms_inv, 2)
            nc.scalar.activation(stat[:, 1, 6:8], stat[:, 1, 4:6], ACT.Sqrt).then_inc(rms_ready, 1)
            act.wait_ge(rms_ready, 2)
            with act.Fori(0, QUARTERS) as q:
                for u in range(QU):
                    v = U_MLP + u
                    split(v + LEAD, q, QU)
                    if u % UPS == UPS - 1 and u < DS * UPS:
                        k = u // UPS
                        for t in range(TT):
                            evac(un[:, t, :], q * QU + (v + 1), k % 2, t, ACT.Relu, scale=stat[:, 1, 6 + t:7 + t])
                    if u % UPS == 2 and UPS < u < DS * UPS + UPS:
                        k = u // UPS - 1
                        for b in range(2):
                            act.wait_ge(tr_full, q * 8 + (R_U + 2 * k + b + 1))
                            nc.scalar.activation(u_hi[:, (4 * k + 2 * b) * T:(4 * k + 2 * b + 2) * T],
                                                 side[:, (R_U + 2 * k + b) % 4, :], ACT.Copy).then_inc(tr_hi, 1)

            def squares(k, t, n):
                act.wait_ge(rms_sum, n)
                nc.scalar.activation(square2[:, :], x_res[:, t, k * SW:(k + 1) * SW], ACT.Square,
                                     accum_out=stat[:, 2 + t, k:k + 1]).then_inc(rms_sum, 1)

            for b in range(4):
                turned(R_X2 + b, a_hi, None, 2 * b)
            for u in range(DS * UPS):
                splits(U_GLU, u)
                if u < 4:
                    turned(R_X2 + 4 + u, a_hi, None, 8 + 2 * u)
                if u % UPS == UPS - 1 and u < DS * UPS - 1:
                    k = u // UPS
                    act.wait_ge(units_used, U_GLU + u + 1)
                    if k >= 2:
                        act.wait_ge(glu_sum, k - 1)
                    sg = (un, usq)[k % 2]
                    nc.scalar.activation(sg[:, :, :], acc[:, 2 * (k % 2):2 * (k % 2) + 2, :], ACT.Sigmoid).then_inc(glu_sig, 1)
                if u % UPS == 2 and u > UPS:
                    k = u // UPS - 1
                    act.wait_ge(glu_sum, k + 1)
                    for t in range(TT):
                        squares(k, t, 4 + TT * k + t)
            for t in range(TT):
                if t == 0:
                    act.wait_ge(fin_first, 1)
                else:
                    act.wait_ge(units_used, U_END)
                nc.scalar.activation(usq[:, t, :], acc[:, 2 + t, :], ACT.Sigmoid).then_inc(glu_sig, 1)
                nc.scalar.activation(stat[:, 3, 4 + t:5 + t], stat[:, 1, 4:5], ACT.Sqrt)
                act.wait_ge(glu_sum, DS + t)
                squares(DS - 1, t, 4 + TT * (DS - 1) + t)
                act.wait_ge(rms_inv, 3 + t)
                nc.scalar.activation(stat[:, 2, 6 + t:7 + t], stat[:, 2, 4 + t:5 + t], ACT.Sqrt).then_inc(rms_ready, 1)
                if t == 0:
                    nc.scalar.activation(stat[:, 3, 6:7], stat[:, 1, 4:5], ACT.Sigmoid)
            act.wait_ge(fin_gain, TT * (DS - 1))
            act.wait_ge(rms_ready, 4)
            for k in range(2):
                strip = slice(k * SW, (k + 1) * SW)
                nc.scalar.activation(ple[:, 1, strip], ple[:, 1, strip], ACT.Copy, scale=stat[:, 2, 7:8]).then_inc(fin_act, 1)

        @block.vector
        def _(dve):
            def split(us, i=0, step=0):
                dve.wait_ge(hi_done, i * step + (us + 1))
                nc.vector.tensor_tensor(w_lo[:, us % SPL, :, :], raw[:, us % RAW, :, :],
                                        w_hi[:, us % SPL, :, :].bitcast(F32), ALU.subtract).then_inc(lo_done, 1)

            def turned(r, hi, lo, col=None, kt=0):
                dve.wait_ge(tr_hi, r + 1)
                b = r % 4
                for kk in range(2):
                    if col is None and kk:
                        break
                    n = 2 * T if col is None else T
                    a = (kt + kk) * T
                    src = side[:, b, kk * T:kk * T + n]
                    if col is None:
                        ins = nc.vector.tensor_tensor(lo[:, a:a + n], src, hi[:, a:a + n].bitcast(F32), ALU.subtract)
                    else:
                        c = col + kt + kk
                        ins = nc.vector.scalar_tensor_tensor(out=lo[:, a:a + n], in0=src, scalar=gT[:, c:c + 1],
                                                             in1=hi[:, a:a + n].bitcast(F32), op0=ALU.mult, op1=ALU.subtract)
                ins.then_inc(tr_lo, 1)

            def inverse_mean(row, n):
                nc.vector.tensor_scalar(stat[:, row, 2:4], stat[:, row, 0:2], 1.0 / D, EPS,
                                        ALU.mult, ALU.add).then_inc(rms_mean, 1)
                dve.wait_ge(rms_mean, n)
                nc.vector.reciprocal(stat[:, row, 4:6], stat[:, row, 2:4]).then_inc(rms_inv, 1)

            def gated(base, kind, k):
                dve.wait_ge(units_used, base + 4 * (k + 1))
                for t in range(TT):
                    nc.vector.tensor_tensor(gate(kind, k)[:, t, :], acc[:, 2 * (k % 2) + t, :], gate(kind, k)[:, t, :],
                                            ALU.mult).then_inc((free0, free1)[t], 1)

            def added(used, k):
                dve.wait_ge(units_used, used)
                for t in range(TT):
                    xs = x_res[:, t, k * SW:(k + 1) * SW]
                    nc.vector.tensor_tensor(xs, acc[:, 2 * (k % 2) + t, :], xs, ALU.add).then_inc((free0, free1)[t], 1)

            dve.wait_ge(g_turned, 1)
            nc.vector.tensor_copy(gT[:, 0:KT], acc[:, 3, 0:KT]).then_inc(g_ready, 1)
            dve.wait_ge(g_ready, 1)
            turned(0, a_hi, a_lo, 0, 0)
            split(0)
            turned(1, a_hi, a_lo, 0, 2)
            split(1)
            split(2)

            def qkv_evac(i, j):
                dve.wait_ge(units_used, i * PAIR + (j + 1) * UPS)
                nc.vector.tensor_scalar(qkv[:, ds(i * HW + (3 * HW + j * SW), SW)], acc[:, 2 * j + 1, :],
                                        stat[:, 0, 7:8], None, ALU.mult).then_inc(free1, 1)

            for u in range(PAIR):
                split(u + LEAD)
                if u < 6:
                    turned(2 + u, a_hi, a_lo, 0, 4 + 2 * u)
                if u == 6:
                    dve.wait_ge(g_turned, 2)
                    nc.vector.tensor_copy(gT[:, KT:G_COLS], acc[:, 3, 0:G_COLS - KT]).then_inc(g_ready, 1)
                    dve.wait_ge(g_ready, 2)
                    dve.wait_ge(rms_sum, 2)
                    inverse_mean(0, 1)
                    l0, l1 = gT[:, G_COLS - 2 * HEADS:G_COLS - HEADS], gT[:, G_COLS - HEADS:G_COLS]
                    nc.vector.tensor_tensor(lb_s[:, 2, :], l0, l1, ALU.max).then_inc(lb_vec, 1)
                    dve.wait_ge(lb_vec, 1)
                    nc.vector.tensor_tensor(lb2[:, 0, :], l0, lb_s[:, 2, :], ALU.subtract)
                    nc.vector.tensor_tensor(lb2[:, 1, :], l1, lb_s[:, 2, :], ALU.subtract).then_inc(lb_vec, 1)
                if u == 9:
                    dve.wait_ge(lb_exp, 1)
                    nc.vector.tensor_tensor(lb_s[:, 2, :], lb_s[:, 0, :], lb_s[:, 1, :], ALU.add).then_inc(lb_vec, 1)
                    dve.wait_ge(lb_vec, 3)
                    nc.vector.reciprocal(lb_s[:, 3, :], lb_s[:, 2, :]).then_inc(lb_vec, 1)
                    dve.wait_ge(lb_vec, 4)
                    nc.vector.tensor_tensor(lbT[:, 0, :], lb_s[:, 0, :], lb_s[:, 3, :], ALU.mult).then_inc(lb_vec, 1)
                    dve.wait_ge(lb_vec, 5)
                    nc.vector.tensor_scalar(lbT[:, 1, :], lbT[:, 0, :], -1.0, 1.0, ALU.mult, ALU.add).then_inc(lb_vec, 1)
                if u == 7:
                    dve.wait_ge(rms_ready, 1)
                if u % UPS == UPS - 1:
                    qkv_evac(0, u // UPS)
            with dve.Fori(1, 3) as i:
                for u in range(PAIR):
                    split(u + LEAD, i, PAIR)
                    if u % UPS == UPS - 1:
                        qkv_evac(i, u // UPS)

            with dve.Fori(0, 4) as i:
                for j in range(2):
                    h = i * 2 + j
                    dve.wait_ge(sb_q, h + 1)
                    nc.vector.tensor_copy(sb_kT[:, :], side[:, 0, T:2 * T]).then_inc(sb_k, 1)
                    for u in range(UPS):
                        v = U_HGP + j * UPS + u
                        split(v + LEAD, i, PAIR)
                        if u == 0:
                            dve.wait_ge(sb_soft, h * 3 + 3)
                            nc.vector.scalar_tensor_tensor(out=sp[:, :], in0=side[:, 1, 0:3 * P], scalar=0.0, in1=sp[:, :],
                                                           op0=ALU.max, op1=ALU.add).then_inc(sb_keep, 1)
                        if u == 4:
                            dve.wait_ge(sb_hi, h + 1)
                            nc.vector.tensor_tensor(b_lo[:, ds(h * T, T)], side[:, 3, 0:T],
                                                    b_hi[:, ds(h * T, T)].bitcast(F32), ALU.subtract).then_inc(sb_lo, 1)
                    dve.wait_ge(units_used, i * PAIR + (U_HGP + (j + 1) * UPS))
                    nc.vector.tensor_scalar(hgp[:, ds(i * TT * HW + (HW + j * SW), SW)], acc[:, 2 * j + 1, :],
                                            stat[:, 0, 7:8], None, ALU.mult).then_inc(free1, 1)

            dve.wait_ge(preset, 3)
            with dve.Fori(0, 4) as i:
                for j in range(2):
                    h = i * 2 + j
                    v0 = h * V_STEPS

                    def take_scores(n):
                        dve.wait_ge(hg_vec, v0 + v_s(n))
                        dve.nop(nofuse=True)
                        bank, at_bank = score_place(n)
                        if n == 0:
                            nc.vector.copy_predicated(score[:, :], masks[:, 0:T], side[:, bank, 0:T]).then_inc(hg_vec, 1)
                            return
                        m = 1 << (n - 1)
                        at_mask = T + (n - 1) * P
                        mask, data = (v.rearrange("p (b m) -> p b m", m=m) for v in (
                            masks[:, at_mask:at_mask + P], side[:, bank, at_bank:at_bank + P]))
                        nc.vector.copy_predicated(even_odd(score[:, :], m)[1], mask, data).then_inc(hg_vec, 1)

                    for u in range(UPS):
                        v = U_GAT + j * UPS + u
                        split(v + LEAD, i, PAIR)
                        if u == 1:
                            dve.wait_ge(hg_q, h + 1)
                            dve.wait_ge(hg_prep, h * 2 + 1)
                            nc.vector.tensor_scalar(t_lev[0][:, :], side[:, 0, 0:T], lb_h[:, 1, :], lb_h[:, 0, :],
                                                    ALU.mult, ALU.add).then_inc(hg_vec, 1)
                            dve.wait_ge(hg_vec, v0 + V_F)
                            nc.vector.tensor_scalar(k_lev[:, 0, :], t_lev[0][:, :], -1.0, 1.0,
                                                    ALU.mult, ALU.add).then_inc(hg_vec, 1)
                            nc.vector.tensor_tensor(q_lev[:, 0, :], side[:, 0, T:2 * T], t_lev[0][:, :],
                                                    ALU.mult).then_inc(hg_vec, 1)
                            for lev in range(7):
                                dve.wait_ge(hg_vec, v0 + v_q(lev))
                                if lev < 6:
                                    tv = t_lev[lev][:, :].rearrange("p (b two) -> p b two", two=2)
                                    nc.vector.tensor_tensor(t_lev[lev + 1][:, :].unsqueeze(2), tv[:, :, 0:1], tv[:, :, 1:2],
                                                            ALU.mult).then_inc(hg_vec, 1)
                                src, dst = (even_odd(q_lev[:, lv, :], 1 << lev) for lv in (lev, lev + 1))
                                nc.vector.tensor_tensor(dst[1], src[1], totals(lev)[0], ALU.mult).then_inc(hg_vec, 1)
                                nc.vector.tensor_copy(dst[0], src[0]).then_inc(hg_vec, 1)
                        if u == 3:
                            dve.wait_ge(hg_s1, h + 1)
                            for n in range(4):
                                take_scores(n)
                        if u == 5:
                            dve.wait_ge(hg_s2, h + 1)
                            for n in range(4, 8):
                                take_scores(n)

            def splits(base, u):
                if base + u + LEAD < U_END:
                    split(base + u + LEAD)

            for u in range(PAIR):
                splits(U_WSB, u)
                if u == 1:
                    dve.wait_ge(hn_sq, 1)
                    nc.vector.tensor_reduce(stat_h[:, 0, :], hgf.rearrange("p (g c) -> p g c", c=P), AXX,
                                            ALU.add).then_inc(hn_mean, 1)
                    dve.wait_ge(hn_mean, 1)
                    nc.vector.tensor_scalar(stat_h[:, 0, :], stat_h[:, 0, :], 1.0 / P, EPS, ALU.mult, ALU.add).then_inc(hn_mean, 1)
                    dve.wait_ge(hn_mean, 2)
                    nc.vector.reciprocal(stat_h[:, 1, :], stat_h[:, 0, :]).then_inc(hn_inv, 1)
                if u == 4:
                    dve.wait_ge(hn_rstd, 1)
                    nc.vector.tensor_tensor(hgy.rearrange("p (g c) -> p g c", c=P), hgo.rearrange("p (g c) -> p g c", c=P),
                                            stat_h[:, 2, :].unsqueeze(2).to_broadcast([P, TT * HEADS, P]),
                                            ALU.mult).then_inc(hn_mul, 1)
                if 9 <= u < 13:
                    turned(R_HG + u - 9, b_hi, b_lo, 2 * KT - HEADS, HEADS + 2 * (u - 9))
                if u % 4 == 3:
                    gated(U_WSB, 0, u // 4)
            for u in range(PAIR):
                splits(U_WHG, u)
                if u in (6, 10, 14):
                    k = (u - 6) // 4
                    for b in range(2):
                        turned(R_Y + 2 * k + b, a_hi, a_lo, None, 4 * k + 2 * b)
                if u % 4 == 3:
                    gated(U_WHG, 1, u // 4)
            for u in range(DS * UPS):
                splits(U_OUT, u)
                if u == 2:
                    for b in range(2):
                        turned(R_Y + 6 + b, a_hi, a_lo, None, 12 + 2 * b)
                if u in (10, 18, 26):
                    k = (u - 10) // 8
                    for b in range(2):
                        turned(R_X1 + 2 * k + b, b_hi, b_lo, KT, 4 * k + 2 * b)
                if u == 28:
                    turned(R_P, u_hi, u_lo)
                if u % UPS == UPS - 1:
                    if u < UPS:
                        dve.wait_ge(xres_in, 16)
                    added(U_OUT + u + 1, u // UPS)
            for u in range(DS):
                splits(U_PLE, u)
                if u == 1:
                    for b in range(2):
                        turned(R_X1B + b, b_hi, b_lo, KT, 12 + 2 * b)
                dve.wait_ge(units_used, U_PLE + u + 1)
                nc.vector.tensor_copy(ple[:, 1, u * SW:(u + 1) * SW], acc[:, 2 * (u % 2) + 1, :]).then_inc(free1, 1)
            dve.wait_ge(rms_sum, 4)
            inverse_mean(1, 2)
            with dve.Fori(0, QUARTERS) as q:
                for u in range(QU):
                    v = U_MLP + u
                    split(v + LEAD, q, QU)
                    if u % UPS == 2 and UPS < u < DS * UPS + UPS:
                        k = u // UPS - 1
                        for b in range(2):
                            a, r = (4 * k + 2 * b) * T, R_U + 2 * k + b
                            dve.wait_ge(tr_hi, q * 8 + (r + 1))
                            nc.vector.tensor_tensor(u_lo[:, a:a + 2 * T], side[:, r % 4, :], u_hi[:, a:a + 2 * T].bitcast(F32),
                                                    ALU.subtract).then_inc(tr_lo, 1)
                    if u % UPS == UPS - 1 and u >= DS * UPS:
                        added(q * QU + (v + 1), u // UPS - DS)
            for b in range(4):
                turned(R_X2 + b, a_hi, a_lo, None, 2 * b)
            for u in range(DS * UPS):
                splits(U_GLU, u)
                if u < 4:
                    turned(R_X2 + 4 + u, a_hi, a_lo, None, 8 + 2 * u)
                if u % UPS == UPS - 1 and u < DS * UPS - 1:
                    k = u // UPS
                    sg = (un, usq)[k % 2]
                    xs = x_res[:, :, k * SW:(k + 1) * SW]
                    dve.wait_ge(glu_sig, k + 1)
                    nc.vector.tensor_tensor(sg[:, :, :], sg[:, :, :], ple[:, :, k * SW:(k + 1) * SW], ALU.mult).then_inc(glu_mul, 1)
                    dve.wait_ge(glu_mul, k + 1)
                    nc.vector.tensor_tensor(xs, xs, sg[:, :, :], ALU.add).then_inc(glu_sum, 1)
            last, third = slice((DS - 1) * SW, D), slice((DS - 2) * SW, (DS - 1) * SW)
            for t in range(TT):
                dve.wait_ge(glu_sig, DS + t)
                nc.vector.tensor_tensor(usq[:, t, :], usq[:, t, :], ple[:, t, last], ALU.mult).then_inc(glu_mul, 1)
                dve.wait_ge(glu_mul, DS + t)
                nc.vector.tensor_tensor(x_res[:, t, last], x_res[:, t, last], usq[:, t, :], ALU.add).then_inc(glu_sum, 1)
                dve.wait_ge(rms_sum, 4 + TT * (DS - 1) + t + 1)
                nc.vector.tensor_reduce(stat[:, 0, t:t + 1], stat[:, 2 + t, 0:DS], AXX, ALU.add).then_inc(rms_mean, 1)
                dve.wait_ge(rms_mean, 2 * t + 3)
                nc.vector.tensor_scalar(stat[:, 0, 2 + t:3 + t], stat[:, 0, t:t + 1], 1.0 / D, EPS,
                                        ALU.mult, ALU.add).then_inc(rms_mean, 1)
                dve.wait_ge(rms_mean, 2 * t + 4)
                nc.vector.reciprocal(stat[:, 2, 4 + t:5 + t], stat[:, 0, 2 + t:3 + t]).then_inc(rms_inv, 1)
                dve.wait_ge(rms_ready, 3 + t)
                rstd = stat[:, 2, 6 + t:7 + t]
                nc.vector.scalar_tensor_tensor(out=x_res[:, t, last], in0=x_res[:, t, last], scalar=rstd, in1=g_fin_b[:, last],
                                               op0=ALU.mult, op1=ALU.mult).then_inc(fin_vec, 1)
                if t == 0:
                    dve.wait_ge(fin_gain, TT * (DS - 1))
                nc.vector.tensor_scalar(ple[:, t, third], ple[:, t, third], rstd, None, ALU.mult).then_inc(fin_vec, 1)

        @block.tensor
        def _(pe):
            def products(us, par, hi, lo, kt, first, last, tiles, kk):
                for t in tiles:
                    a = (kt + kk) * T + t * P
                    terms = ((hi, w_hi), (hi, w_lo), (lo, w_hi))
                    for s, (act_part, w_part) in enumerate(terms):
                        ins = nc.tensor.matmul(acc[:, 2 * par + t, :], act_part[:, a:a + P], w_part[:, us % SPL, kk, :],
                                               start=first and kk == 0 and s == 0,
                                               stop=last and kk == UK - 1 and s == 2)
                return ins

            def unit(n, us, g, par, hi, lo, kt, first, last):
                pe.wait_ge(lo_done, n + 1)
                if first and g is not None:
                    pe.wait_ge(free0, g - 1)
                    pe.wait_ge(free1, g - 1)
                for kk in range(UK):
                    ins = products(us, par, hi, lo, kt, first, last, range(TT), kk)
                ins.then_inc(units_used, 1)

            def turn(r, b, src, kt, ready=None):
                if ready is not None:
                    pe.wait_ge(tr_lo, ready)
                for kk in range(2):
                    for t in range(TT):
                        ins = nc.tensor.transpose(side[:, b, kk * T + t * P:kk * T + (t + 1) * P],
                                                  src(t, kt + kk), ident[:, :])
                ins.then_inc(tr_full, 1)

            def turn_static(r, src, kt):
                turn(r, r % 4, src, kt, r - 3 if r >= 4 else None)

            def cols(tl):
                return lambda t, kt: tl[:, t, kt * P:(kt + 1) * P]

            def keep_warm(n):
                for _ in range(n):
                    nc.tensor.matmul(acc[:, 2, 0:P], nones[:, :], nones[:, :], start=True, stop=True)

            pe.wait_ge(preset, 1)
            keep_warm(5)
            pe.wait_ge(ident_in, 16)
            pe.wait_ge(g_first_in, 16)
            nc.tensor.transpose(acc[:, 3, 0:P], g_first[:, :], ident[:, :]).then_inc(g_turned, 1)
            for r in range(2):
                keep_warm(1 + 3 * r)
                pe.wait_ge(x_piece[r], 16)
                turn_static(r, cols(x_in), 2 * r)
            keep_warm(6)
            for u in range(PAIR):
                if u < 8:
                    pe.wait_ge(tr_lo, u + 1)
                if u == UPS:
                    pe.wait_ge(g_ready, 2)
                unit(u, u, None, u // UPS, a_hi, a_lo, u % UPS * UK, u % UPS == 0, u % UPS == UPS - 1)
                if u < 6:
                    if u % 2 == 0:
                        pe.wait_ge(x_piece[u // 2 + 2], 16)
                    turn_static(2 + u, cols(x_in), 4 + 2 * u)
                if u == 6:
                    pe.wait_ge(g_in, 3 * 16)
                    nc.tensor.transpose(acc[:, 3, 0:P], g_rows[:, :], ident[:, :]).then_inc(g_turned, 1)
            with pe.Fori(1, 3) as i:
                for u in range(PAIR):
                    j = u // UPS
                    unit(i * PAIR + u, u, i * 2 + j, j, a_hi, a_lo, u % UPS * UK, u % UPS == 0, u % UPS == UPS - 1)

            pe.wait_ge(preset, 1)
            pe.wait_ge(tables_in, 32)
            with pe.Fori(0, 4) as i:
                for j in range(2):
                    h = i * 2 + j
                    st = stage[j]
                    pe.wait_ge(sb_staged, h + 1)
                    for kind in range(2):
                        for t in range(TT):
                            ins = nc.tensor.transpose(side[:, 0, kind * T + t * P:kind * T + (t + 1) * P],
                                                      st[:, t, kind, :], ident[:, :])
                    ins.then_inc(sb_turned, 1)
                    for u in range(UPS):
                        v = U_HGP + j * UPS + u
                        unit(i * PAIR + v, v, i * 2 + (G_HGP + j), j, a_hi, a_lo, u * UK, u == 0, u == UPS - 1)
                        if u == 0:
                            pe.wait_ge(sb_q, h + 1)
                            pe.wait_ge(sb_k, h + 1)
                            nc.tensor.matmul(side[:, 1, 0:T], sb_kT[:, 0:P], sb_qT[:, :], start=True, stop=False,
                                             skip_group_check=True)
                            nc.tensor.matmul(side[:, 1, T:T + P], sb_kT[:, P:T], sb_qT[:, P:T], start=False, stop=False,
                                             skip_group_check=True).then_inc(sb_z, 1)
                        if u == 2:
                            pe.wait_ge(sb_masked, h + 1)
                            nc.tensor.matmul(side[:, 1, 0:T], ntri[:, :], sp[:, 0:T], start=False, stop=False,
                                             skip_group_check=True)
                            nc.tensor.matmul(side[:, 1, P:T], nones[:, :], sp[:, T:T + P], start=False, stop=False,
                                             skip_group_check=True)
                            nc.tensor.matmul(side[:, 1, T:T + P], ntri[:, :], sp[:, T:T + P], start=False, stop=True,
                                             skip_group_check=True).then_inc(sb_later, 1)
                        if u == 4:
                            pe.wait_ge(sb_wm, h + 1)
                            nc.tensor.matmul(side[:, 3, 0:T], st[:, 0, 2, :], wt[:, 0:T], start=True, stop=False)
                            nc.tensor.matmul(side[:, 3, P:T], st[:, 1, 2, :], wt[:, T:T + P], start=False,
                                             stop=True).then_inc(sb_o, 1)

            pe.wait_ge(preset, 3)
            with pe.Fori(0, 4) as i:
                for j in range(2):
                    h = i * 2 + j
                    v0, g0 = h * V_STEPS, h * G_STEPS
                    def level(n):
                        bank, at_bank = score_place(n)
                        for t in range(TT):
                            tokens = slice(t * P, (t + 1) * P)
                            if n == 0:
                                ins = nc.tensor.matmul(side[:, bank, tokens], k_lev[:, 0, tokens], q_dia[:, tokens],
                                                       start=True, stop=True)
                                continue
                            m, a = 1 << (n - 1), at_bank + t * P // 2
                            ins = nc.tensor.matmul(side[:, bank, a:a + P // 2].rearrange("p (b m) -> p b m", m=m),
                                                   k_lev[:, n - 1, tokens], even_odd(q_lev[:, n - 1, tokens], m)[1],
                                                   start=True, stop=True)
                        return ins

                    for u in range(UPS):
                        v = U_GAT + j * UPS + u
                        unit(i * PAIR + v, v, i * 2 + (G_GAT + j), j, a_hi, a_lo, u * UK, u == 0, u == UPS - 1)
                        if u == 1:
                            pe.wait_ge(hg_prep, h * 2 + 1)
                            for t in range(TT):
                                nc.tensor.transpose(side[:, 0, t * P:(t + 1) * P], s_f[:, t, :], ident[:, :])
                                ins = nc.tensor.transpose(side[:, 0, T + t * P:T + (t + 1) * P], st_q[:, t, :], ident[:, :])
                            ins.then_inc(hg_turned, 1)
                        if u == 3:
                            pe.wait_ge(hg_q, h + 1)
                            pe.wait_ge(hg_vec, v0 + v_q(2))
                            pe.wait_ge(hg_key, g0 + 4)
                            for n in range(4):
                                ins = level(n)
                            ins.then_inc(hg_s1, 1)
                        if u == 5:
                            pe.wait_ge(hg_vec, v0 + v_q(7))
                            pe.wait_ge(hg_key, g0 + G_STEPS)
                            for n in range(4, 8):
                                level(n)
                            nc.tensor.matmul(side[:, 0, 0:P], k_lev[:, 7, 0:P], q_lev[:, 7, P:T], start=True,
                                             stop=True).then_inc(hg_s2, 1)
                        if u == 7:
                            pe.wait_ge(hg_vec, v0 + v_s(8))
                            pe.wait_ge(hg_cross, h + 1)
                            vh = [hgp_v[:, 1, t, ds(h * P, P)] for t in range(TT)]
                            nc.tensor.matmul(side[:, 2, 0:P], score[:, 0:P], vh[0], start=True, stop=True)
                            nc.tensor.matmul(side[:, 2, P:T], cross[:, :], vh[0], start=True, stop=False)
                            nc.tensor.matmul(side[:, 2, P:T], score[:, P:T], vh[1], start=False, stop=True).then_inc(hg_o, 1)

            hgy_v = hgy.rearrange("p (t c) -> p t c", t=TT)
            pe.wait_ge(sb_lo, HEADS)
            for u in range(PAIR):
                unit(U_WSB + u, U_WSB + u, G_WSB + u // 4, u // 4 % 2, b_hi, b_lo, u % 4 * UK, u % 4 == 0, u % 4 == 3)
                if 9 <= u < 13:
                    pe.wait_ge(hn_y, 1)
                    turn_static(R_HG + u - 9, cols(hgy_v), 2 * (u - 9))

            def y_cols(t, kt):
                return gate(0, kt // 4)[:, t, kt % 4 * P:(kt % 4 + 1) * P]

            for u in range(PAIR):
                if u < 4:
                    pe.wait_ge(tr_lo, R_HG + u + 1)
                unit(U_WHG + u, U_WHG + u, G_WHG + u // 4, u // 4 % 2, b_hi, b_lo, HEADS + u % 4 * UK, u % 4 == 0, u % 4 == 3)
                if u in (6, 10, 14):
                    k = (u - 6) // 4
                    pe.wait_ge(y_ready, k + 1)
                    for b in range(2):
                        turn_static(R_Y + 2 * k + b, y_cols, 4 * k + 2 * b)
            for u in range(DS * UPS):
                if u < UPS:
                    pe.wait_ge(tr_lo, R_Y + u + 1)
                unit(U_OUT + u, U_OUT + u, G_OUT + u // UPS, u // UPS % 2, a_hi, a_lo, u % UPS * UK, u % UPS == 0,
                     u % UPS == UPS - 1)
                if u == 2:
                    pe.wait_ge(y_ready, 4)
                    for b in range(2):
                        turn_static(R_Y + 6 + b, y_cols, 12 + 2 * b)
                if u in (10, 18, 26):
                    k = (u - 10) // 8
                    pe.wait_ge(free1, G_OUT + k + 1)
                    for b in range(2):
                        turn_static(R_X1 + 2 * k + b, cols(x_res), 4 * k + 2 * b)
                if u == 28:
                    pe.wait_ge(p_in_s, 16)
                    turn_static(R_P, cols(p_in), 0)
            for u in range(DS):
                if u == 0:
                    pe.wait_ge(tr_lo, R_P + 1)
                unit(U_PLE + u, U_PLE + u, G_PLE + u, u % 2, u_hi, u_lo, 0, True, True)
                if u == 1:
                    pe.wait_ge(free1, G_OUT + 4)
                    for b in range(2):
                        turn_static(R_X1B + b, cols(x_res), 12 + 2 * b)
            with pe.Fori(0, QUARTERS) as q:
                for u in range(QU):
                    v, k = U_MLP + u, u // UPS
                    if k == 0:
                        pe.wait_ge(tr_lo, R_U)
                    if k == DS:
                        pe.wait_ge(tr_lo, q * 8 + (R_U + u % UPS + 1))
                    hi, lo = (b_hi, b_lo) if k < DS else (u_hi, u_lo)
                    unit(q * QU + v, v, q * 2 * DS + (G_MLP + k), k % 2, hi, lo, u % UPS * UK, u % UPS == 0, u % UPS == UPS - 1)
                    if u % UPS == 2 and UPS < u < DS * UPS + UPS:
                        k -= 1
                        pe.wait_ge(usq_done, q * DS + (k + 1))
                        for b in range(2):
                            r = R_U + 2 * k + b
                            turn(r, r % 4, lambda t, kt: usq[:, t, kt * P:(kt + 1) * P], 2 * b, q * 8 + (r - 3))
            for b in range(4):
                turn_static(R_X2 + b, cols(x_res), 2 * b)
            for u in range(DS * UPS - SPL):
                if u < UPS:
                    pe.wait_ge(tr_lo, R_X2 + u + 1)
                if u // UPS >= 2 and u % UPS == 0:
                    pe.wait_ge(glu_sig, u // UPS - 1)
                unit(U_GLU + u, U_GLU + u, G_GLU + u // UPS if u // UPS < 2 else None, u // UPS % 2, a_hi, a_lo,
                     u % UPS * UK, u % UPS == 0, u % UPS == UPS - 1)
                if u < 4:
                    if u == 2:
                        pe.wait_ge(free1, G_GLU)
                    turn_static(R_X2 + 4 + u, cols(x_res), 8 + 2 * u)
            for t in range(TT):
                for u in range(UPS - SPL, UPS):
                    n = U_GLU + (DS - 1) * UPS + u
                    if t == 0:
                        pe.wait_ge(lo_done, n + 1)
                    for kk in range(UK):
                        ins = products(n, (DS - 1) % 2, a_hi, a_lo, u * UK, False, u == UPS - 1, (t,), kk)
                    if t:
                        ins.then_inc(units_used, 1)
                if t == 0:
                    ins.then_inc(fin_first, 1)


def kernel(x, p, mix_norm_g, w_in, hgrn_lb_logits, hgrn_out_norm_g, w_o_sb, w_o_hg, w_out, mlp_norm_g, w_up, w_down,
           w_ple_proj, w_ple_gate, final_norm_g):
    import concourse.bacc as bacc
    from concourse.bass_utils import run_bass_kernel_spmd

    row = np.arange(P)
    key, query = row[:, None], row[None, :]
    levels = [key == query]
    for j in range(LEVELS - 1):
        m = 1 << j
        odd = query[:, row // m % 2 == 1]
        levels.append(key // m == odd // m - 1)
    masks = np.concatenate([np.tile(lv, (1, TT)) for lv in levels], axis=1).astype(np.float32)
    arrays = {
        "x": x[0], "p": p[0, 0], "g_mix": mix_norm_g, "w_in": w_in[0], "lb_logits": hgrn_lb_logits,
        "g_hg": hgrn_out_norm_g, "w_o_sb": w_o_sb[0], "w_o_hg": w_o_hg[0], "w_out": w_out[0], "g_mlp": mlp_norm_g,
        "w_up": w_up[0], "w_down": w_down[0], "w_ple": w_ple_proj[0], "w_glu": w_ple_gate[0], "g_fin": final_norm_g,
        "c_ident": np.eye(P, dtype=np.float32), "c_ntri": -(key >= query).astype(np.float32), "c_masks": masks,
    }
    nc = bacc.Bacc("TRN2", target_bir_lowering=False, num_devices=1)
    maps, args = {}, []
    for name, a in arrays.items():
        a = np.ascontiguousarray(a)
        maps[f"in_{name}"] = a
        args.append(nc.dram_tensor(f"in_{name}", a.shape, mybir.dt.from_np(a.dtype), kind="ExternalInput").ap())
    args.append(nc.dram_tensor("out_0", (T, D), F32, kind="ExternalOutput").ap())
    build(nc, *args)
    result = run_bass_kernel_spmd(nc, [maps], core_ids=[0])
    return result.results[0]["out_0"].reshape(x.shape)
```
